# Optimizing a Trainium2 kernel written in Bass

```python
import jax, jax.numpy as jnp
from jax import lax
import numpy as np

D_MODEL = 2048
BATCH = 1
SEQ = 512
DEPTH = 1

CHUNK = 64
W_A = D_MODEL // 2
W_B = D_MODEL // 2
D_MIX = W_A + W_B
H_A = 8
D_K = W_A // H_A
D_V = W_A // H_A
CONV_WIDTH = 31
N_IN = 4 * W_A + 3 * W_B
EPS = 1e-6
LB_FLOOR = 1e-30

kernel_name = "hgrn2_conformer_hybrid_trunk"

def rmsnorm(x, g):
    xf = x.astype(jnp.float32)
    y = xf * lax.rsqrt(jnp.mean(xf * xf, axis=-1, keepdims=True) + EPS)
    return (y * g.astype(jnp.float32)).astype(x.dtype)

def layernorm(x, g, b):
    xf = x.astype(jnp.float32)
    mu = jnp.mean(xf, axis=-1, keepdims=True)
    var = jnp.mean(jnp.square(xf - mu), axis=-1, keepdims=True)
    y = (xf - mu) * lax.rsqrt(var + EPS)
    return (y * g.astype(jnp.float32) + b.astype(jnp.float32)).astype(x.dtype)

def layer_lower_bounds(lb_logits):
    p = jax.nn.softmax(lb_logits.astype(jnp.float32), axis=0)
    return jnp.cumsum(p, axis=0) - p[0:1]

def hgrn2_mixer(q, fz, iv, lb, norm_g):
    B, T, _ = q.shape
    nc = T // CHUNK

    def heads(u, d):
        return u.astype(jnp.float32).reshape(B, nc, CHUNK, H_A, d).transpose(1, 0, 3, 2, 4)

    lb_h = lb.astype(jnp.float32).reshape(H_A, 1, D_K)
    zq = heads(q, D_K) * (D_K ** -0.5)
    zf = heads(fz, D_K)
    v = heads(iv, D_V)
    log_lb = jnp.log(jnp.maximum(lb_h, LB_FLOOR))
    log_f = jnp.logaddexp(log_lb, jnp.log1p(-lb_h) + jax.nn.log_sigmoid(zf))
    k = (1.0 - lb_h) * jax.nn.sigmoid(-zf)
    causal = jnp.tril(jnp.ones((CHUNK, CHUNK), dtype=bool))[:, :, None]

    def step(S, inp):
        qc, kc, vc, gc = inp
        b = jnp.cumsum(gc, axis=-2)
        diff = b[..., :, None, :] - b[..., None, :, :]
        decay = jnp.where(causal, jnp.exp(jnp.where(causal, diff, 0.0)), 0.0)
        scores = jnp.einsum('bhtk,bhtsk,bhsk->bhts', qc, decay, kc)
        o = jnp.einsum('bhts,bhsv->bhtv', scores, vc) \
            + jnp.einsum('bhtk,bhkv->bhtv', qc * jnp.exp(b), S)
        b_last = b[..., -1:, :]
        S_new = jnp.exp(b_last[..., 0, :])[..., None] * S \
            + jnp.einsum('bhsk,bhsv->bhkv', kc * jnp.exp(b_last - b), vc)
        return S_new, o

    S0 = jnp.zeros((B, H_A, D_K, D_V), jnp.float32)
    _, o = lax.scan(step, S0, (zq, k, v, log_f))
    o = o.transpose(1, 0, 3, 2, 4).reshape(B, T, H_A, D_V)
    o = o * lax.rsqrt(jnp.mean(o * o, axis=-1, keepdims=True) + EPS) * norm_g.astype(jnp.float32)
    return o.reshape(B, T, W_A).astype(q.dtype)

def conformer_conv(u, ug, dw_k, dw_b, ln_g, ln_b):
    a = u * jax.nn.sigmoid(ug)
    y = lax.conv_general_dilated(
        a, dw_k.astype(a.dtype)[:, None, :],
        window_strides=(1,), padding=[(CONV_WIDTH - 1, 0)],
        dimension_numbers=('NWC', 'WIO', 'NWC'), feature_group_count=W_B)
    y = y + dw_b.astype(y.dtype)
    y = layernorm(y, ln_g, ln_b)
    return jax.nn.silu(y)

def setup_inputs(seed: int = 0) -> dict:
    key = jax.random.key(seed)
    ks = jax.random.split(key, 12)
    f32 = jnp.float32
    x = jax.random.normal(ks[0], (BATCH, SEQ, D_MODEL), f32)
    pre_norm_g = 1.0 + 0.05 * jax.random.normal(ks[1], (DEPTH, D_MODEL), f32)
    post_norm_g = 1.0 + 0.05 * jax.random.normal(ks[2], (DEPTH, D_MODEL), f32)
    w_in = jax.random.normal(ks[3], (DEPTH, D_MODEL, N_IN), f32) * D_MODEL ** -0.5
    lb_logits = 0.5 * jax.random.normal(ks[4], (DEPTH, W_A), f32)
    hg_norm_g = 1.0 + 0.05 * jax.random.normal(ks[5], (DEPTH, D_V), f32)
    dw_kernel = jax.random.normal(ks[6], (DEPTH, CONV_WIDTH, W_B), f32) * CONV_WIDTH ** -0.5
    dw_bias = 0.02 * jax.random.normal(ks[7], (DEPTH, W_B), f32)
    conv_ln_g = 1.0 + 0.05 * jax.random.normal(ks[8], (DEPTH, W_B), f32)
    conv_ln_b = 0.02 * jax.random.normal(ks[9], (DEPTH, W_B), f32)
    w_out = jax.random.normal(ks[10], (DEPTH, D_MIX, D_MODEL), f32) * D_MIX ** -0.5
    return {"x": x, "pre_norm_g": pre_norm_g, "post_norm_g": post_norm_g, "w_in": w_in,
            "lb_logits": lb_logits, "hg_norm_g": hg_norm_g, "dw_kernel": dw_kernel,
            "dw_bias": dw_bias, "conv_ln_g": conv_ln_g, "conv_ln_b": conv_ln_b, "w_out": w_out}

def reference(x, pre_norm_g, post_norm_g, w_in, lb_logits, hg_norm_g, dw_kernel,
              dw_bias, conv_ln_g, conv_ln_b, w_out):
    lower_bounds = layer_lower_bounds(lb_logits)
    split_pts = [W_A, 2 * W_A, 3 * W_A, 4 * W_A, 4 * W_A + W_B, 4 * W_A + 2 * W_B]
    for l in range(DEPTH):
        h = rmsnorm(x, pre_norm_g[l])
        proj = jnp.einsum('btd,dn->btn', h, w_in[l].astype(h.dtype))
        q, fz, iv, gate_a, u, ug, gate_b = jnp.split(proj, split_pts, axis=-1)
        o_a = hgrn2_mixer(q, fz, iv, lower_bounds[l], hg_norm_g[l]) * jax.nn.silu(gate_a)
        o_b = conformer_conv(u, ug, dw_kernel[l], dw_bias[l], conv_ln_g[l], conv_ln_b[l]) \
            * jax.nn.silu(gate_b)
        mixed = jnp.concatenate([o_a, o_b], axis=-1)
        y = jnp.einsum('btm,md->btd', mixed, w_out[l].astype(mixed.dtype))
        x = x + rmsnorm(y, post_norm_g[l])
    return x


_drawn_inputs = setup_inputs


def setup_inputs(seed=0):
    import zlib

    import numpy as np

    out = dict(_drawn_inputs(seed))
    spreads = {}
    factors = {'dw_bias': 3.836, 'conv_ln_g': 2.777, 'conv_ln_b': 7.651}
    for name, (base, spread) in spreads.items():
        noise = np.random.default_rng([zlib.crc32(name.encode()), seed]).standard_normal(out[name].shape)
        drawn = base * np.exp(spread * noise) if base else spread * noise
        out[name] = __import__('jax').numpy.asarray(drawn.astype(out[name].dtype))
    for name, factor in factors.items():
        out[name] = (out[name] * factor).astype(out[name].dtype)
    return out
```

```python
from contextlib import ExitStack

import concourse.bass as bass
from concourse import mybir


def build_layer(nc, x, pre_norm_g, post_norm_g, w_in, lb_logits, hg_norm_g, dw_kernel, dw_bias,
                conv_ln_g, conv_ln_b, w_out, out):
    fp32, fp32r, i8 = mybir.dt.float32, mybir.dt.float32r, mybir.dt.int8
    ALU, ACT, AX = mybir.AluOpType, mybir.ActivationFunctionType, mybir.AxisListType
    ds = bass.ds
    P = 128
    _, T, D = x.shape
    W_A = lb_logits.shape[1]
    W_B = dw_bias.shape[1]
    TAPS = dw_kernel.shape[1]
    H = W_A // P
    J = W_B // P
    KT = D // P
    HK = KT // 2
    TT = T // P
    UW = HK * P
    RING = 4
    EPS, LB_FLOOR = 1e-6, 1e-30
    Q_SCALE = float(P) ** -0.5
    LN2_50 = 34.657359027997264
    AHEAD = 2

    CONV_T, HEAD_T = 3, 4
    CONV_U, HEAD_U = 2 * CONV_T, 2 * HEAD_T
    N_HEAD = J * CONV_U
    N_OUT = N_HEAD + H * HEAD_U
    CHUNKS = D // 512
    OUT_U = (W_A + W_B) // (2 * P)
    N_END = N_OUT + CHUNKS * OUT_U

    COL_Q, COL_F, COL_V, COL_GA = 0, W_A, 2 * W_A, 3 * W_A
    COL_U, COL_UG, COL_GB = 4 * W_A, 4 * W_A + W_B, 4 * W_A + 2 * W_B
    CONV_COLS = (COL_UG, COL_U, COL_GB)
    HEAD_COLS = (COL_F, COL_Q, COL_V, COL_GA)

    LEVELS = [64, 32, 16, 8, 4, 2]
    NL = len(LEVELS)
    HALF = T // 2
    PAIRS = [0, 1, 2] + [H // 2 + q for q in range(J // 2)] + [3]
    MIX_AT = [2 * q + r for q in PAIRS for r in range(2)]

    ctx = ExitStack()
    with ctx:
        def sb(name, shape, dt=fp32):
            return ctx.enter_context(nc.sbuf_tensor(name, shape, dt))

        def sems(names):
            return [ctx.enter_context(nc.semaphore(n)) for n in names.split()]

        h_hi = sb("h_hi", [P, KT * T], fp32r)
        h_lo = sb("h_lo", [P, KT * T], fp32r)
        w_raw = sb("w_raw", [P, RING * UW])
        w_hi = sb("w_hi", [P, RING * UW], fp32r)
        w_lo = sb("w_lo", [P, RING * UW], fp32r)
        mix = sb("mix", [P, KT * T])
        gates = sb("gates", [P, J * T])
        work = sb("work", [P, 21 * T])

        def part(n, k=1):
            return work[:, n * T:(n + k) * T]

        t1, t2, t3, t4 = (part(n) for n in range(4))
        bcum, key, qry, kmod = (part(n) for n in range(4, 8))
        lev = [part(8 + n) for n in range(NL)]
        kdec, qdec, vals, probs, sgate, lnr = (part(n) for n in range(14, 20))
        state = part(20)
        PADW = TAPS - 1 + T
        apad = [work[:, 10 * T + r * PADW:10 * T + (r + 1) * PADW] for r in range(2)]
        glu = kdec
        stage = work[:, 4 * T:4 * T + 3 * P]
        ident = sb("ident", [P, P])
        ones = sb("ones", [P, P])
        mask = sb("mask", [P, (NL + 2) * HALF], i8)
        NPAR = TAPS + 4
        par = sb("par", [P, NPAR * J + 1])
        par3 = par[:, 0:NPAR * J].rearrange("p (n j) -> p n j", j=J)
        HGC = NPAR * J
        tap = sb("tap", [P, 2 * (TAPS + 1)])
        lnp = sb("lnp", [P, 2])
        lbw = sb("lbw", [P, 4 * H])
        lbp = sb("lbp", [P, 3 * H])
        hcur = sb("hcur", [P, 3])
        ebl = sb("ebl", [P, TT])
        ssq = sb("ssq", [P, TT * CHUNKS])
        rst = sb("rst", [P, 2 * TT])
        epsb = sb("epsb", [P, 1])
        EPSB = epsb[:, 0:1]

        banks = ctx.enter_context(nc.psum_tensor("banks", [P, 8 * 512], fp32))

        def bank(n, k=1):
            return banks[:, n * 512:(n + k) * 512]

        LV0, LV1, XB, OB = bank(4), bank(5), bank(6), bank(7)

        (x_in0, x_in1, x_in2, x_in3, gain_in, par_in, res_in, stored) = sems(
            "x_in0 x_in1 x_in2 x_in3 gain_in par_in res_in stored")
        x_in = [x_in0, x_in1, x_in2, x_in3]
        raw_in = sems("raw_in0 raw_in1 raw_in2 raw_in3")
        (hi_done, lo_done, unit_done) = sems("hi_done lo_done unit_done")
        (pool_c, masks_ready, par_t, par_ready, lb_v, lb_s) = sems(
            "pool_c masks_ready par_t par_ready lb_v lb_s")
        (eps_ready, x_ss, x_rst, x_norm, x_tr, x_hi, x_lo) = sems(
            "eps_ready x_ss x_rst x_norm x_tr x_hi x_lo")
        (ug_s, ug_taken, glu_ready, u_taken, gb_taken, tap_ready, tap_done, ysum_done) = sems(
            "ug_s ug_taken glu_ready u_taken gb_taken tap_ready tap_done ysum_done")
        (mean_done, cen_done, csq_done, vacc_done, var_done, lnr_s) = sems(
            "mean_done cen_done csq_done vacc_done var_done lnr_s")
        (ln_x, ln_v, ln_s, ln_sig) = sems("ln_x ln_v ln_s ln_sig")
        (gate_taken, gate_s, gate_ls, gate_sig, gate_ready) = sems(
            "gate_taken gate_s gate_ls gate_sig gate_ready")
        (hc_ready, f_s, f_v, f_la, key_ready, q_taken, v_taken) = sems(
            "hc_ready f_s f_v f_la key_ready q_taken v_taken")
        (lev_d, lev_e, lev_ready, kdec_e, kdec_ready, qdec_e, qdec_ready, ebl_ready) = sems(
            "lev_d lev_e lev_ready kdec_e kdec_ready qdec_e qdec_ready ebl_ready")
        (lev_done, vt_done, vt_taken, kt_done, kt_taken, probs_done) = sems(
            "lev_done vt_done vt_taken kt_done kt_taken probs_done")
        (st_done, st_v, o_done, osq_done, norm_done, rs_s, on_done, head_done) = sems(
            "st_done st_v o_done osq_done norm_done rs_s on_done head_done")
        (mhi_done, mlo_done, y_mm, y_taken, y_sq, y_ssum, y_rs, y_out) = sems(
            "mhi_done mlo_done y_mm y_taken y_sq y_ssum y_rs y_out")

        block = ctx.enter_context(nc.Block())

        def cut(t, m, odd):
            return t.rearrange("p (g two m) -> p g two m", two=2, m=m)[:, :, odd, :]

        def runs(t, m):
            return t.rearrange("p (g m) -> p g m", m=m)

        def held(eng, value):
            return value if isinstance(value, int) else eng.to_reg(value)

        @block.sync
        def _(sp):
            def load_unit(n, slot, src, width):
                sp.dma_start(w_raw[:, slot * UW:(slot + 1) * UW].rearrange("p (k c) -> p k c", c=width),
                             src.rearrange("(k p) c -> p k c", p=P)).then_inc(raw_in[slot], 16)

            def in_unit(n, slot, half, col):
                load_unit(n, slot, w_in[0, half * UW:(half + 1) * UW, ds(col, P)], P)

            def conv_loads(i, first=False):
                for r in range(2):
                    for s in range(CONV_U):
                        m = CONV_U * r + s
                        n = 2 * CONV_U * i + m
                        if not (first and m < RING):
                            cut_before = held(sp, n - RING + 1)
                            sp.wait_ge(raw_in[m % RING], 16)
                            sp.wait_ge(lo_done, cut_before)
                        in_unit(n, m % RING, s % 2, CONV_COLS[s // 2] + (2 * i + r) * P)

            for tt in range(TT):
                sp.dma_start(mix[:, tt * D:(tt + 1) * D], x[0, tt * P:(tt + 1) * P, :]).then_inc(x_in[tt], 16)
                if tt == 0:
                    sp.dma_start(gates[:, 0:D], pre_norm_g[0].partition_broadcast(P)).then_inc(gain_in, 16)
            conv_loads(0, first=True)
            with sp.Fori(1, J // 2) as i:
                conv_loads(i)
            with sp.Fori(0, H) as h:
                for u in range(HEAD_U):
                    n = N_HEAD + HEAD_U * h + u
                    cut_before = held(sp, n - RING + 1)
                    sp.wait_ge(raw_in[u % RING], 16)
                    sp.wait_ge(lo_done, cut_before)
                    in_unit(n, u % RING, u % 2, HEAD_COLS[u // 2] + h * P)
            with sp.Fori(0, CHUNKS) as c:
                for s in range(OUT_U):
                    n = N_OUT + OUT_U * c + s
                    cut_before = held(sp, n - RING + 1)
                    sp.wait_ge(raw_in[s % RING], 16)
                    sp.wait_ge(lo_done, cut_before)
                    load_unit(n, s % RING, w_out[0, 2 * P * PAIRS[s]:2 * P * (PAIRS[s] + 1), ds(c * 512, 512)], 512)
            for tt in range(TT):
                sp.wait_ge(y_out, tt + 1)
                sp.dma_start(out[0, tt * P:(tt + 1) * P, :], mix[:, tt * D:(tt + 1) * D]).then_inc(stored, 16)
            sp.wait_ge(stored, 16 * TT)

        @block.gpsimd
        def _(pool):
            g = nc.gpsimd
            count = [0]

            def link(ins):
                count[0] += 1
                ins.then_inc(pool_c, 1)
                pool.wait_ge(pool_c, count[0])

            link(g.memset(ones[:], 1.0))
            link(g.memset(ident[:], 1.0))
            link(g.affine_select(out=ident[:], in_=ident[:], pattern=[[-1, P]], compare_op=ALU.is_equal,
                                 fill=0.0, base=0, channel_multiplier=1))
            link(g.memset(mask[:], 1))
            for n, m in enumerate(LEVELS + [1, 1]):
                w = mask[:, n * HALF:(n + 1) * HALF].rearrange("p (b g m) -> p b g m", b=TT, m=m)
                top = m - 1 if n < NL else (1, 0)[n - NL]
                link(g.affine_select(out=w, in_=w, pattern=[[0, TT], [-2 * m, P // (2 * m)], [0, m]],
                                     compare_op=ALU.is_ge, fill=0.0, base=0, channel_multiplier=1))
                link(g.affine_select(out=w, in_=w, pattern=[[0, TT], [2 * m, P // (2 * m)], [0, m]],
                                     compare_op=ALU.is_ge, fill=0.0, base=top, channel_multiplier=-1))
            g.memset(probs, 0.0).then_inc(masks_ready, 1)

            with pool.Fori(0, N_END // RING) as i:
                for s in range(RING):
                    pool.wait_ge(hi_done, RING * i + s + 1)
                    a = slice(s * UW, (s + 1) * UW)
                    g.tensor_tensor(w_lo[:, a], w_raw[:, a], w_hi[:, a].bitcast(fp32), ALU.subtract).then_inc(lo_done, 1)

        @block.scalar
        def _(act):
            A = nc.scalar.activation

            def hi_unit(n, slot, q, first=False):
                act.wait_ge(raw_in[slot], 16 * (q + 1))
                if not first:
                    act.wait_ge(unit_done, n - RING + 1)
                a = slice(slot * UW, (slot + 1) * UW)
                A(w_hi[:, a], w_raw[:, a], ACT.Copy).then_inc(hi_done, 1)

            def softplus_of_abs(src, tmp, sem, base):
                A(tmp, src, ACT.Abs).then_inc(sem, 1)
                act.wait_ge(sem, base + 1)
                A(tmp, tmp, ACT.Exp, scale=-1.0).then_inc(sem, 1)
                act.wait_ge(sem, base + 2)
                A(tmp, tmp, ACT.Ln, bias=1.0).then_inc(sem, 1)

            nc.scalar.preload_act_table_set("natural_log_exp_and_others")
            dwr = dw_kernel[0].rearrange("w (j c) -> (w j) c", c=P)
            R1 = TAPS * J - P
            act.dma_start(stage[:, 0:P], dwr[0:P, :]).then_inc(par_in, 16)
            act.dma_start(stage[0:R1, P:2 * P], dwr[P:TAPS * J, :]).then_inc(par_in, 16)
            act.dma_start(stage[R1:R1 + J, P:2 * P], dw_bias[0].rearrange("(j c) -> j c", c=P)).then_inc(par_in, 16)
            for n, v in enumerate((conv_ln_g, conv_ln_b, lb_logits)):
                act.dma_start(stage[n * J:(n + 1) * J, 2 * P:3 * P], v[0].rearrange("(j c) -> j c", c=P)).then_inc(par_in, 16)
            act.dma_start(stage[3 * J:3 * J + 1, 2 * P:3 * P], hg_norm_g).then_inc(par_in, 16)

            def x_stats(tt):
                act.wait_ge(x_in[tt], 16)
                A(gates[:, D:2 * D], mix[:, tt * D:(tt + 1) * D], ACT.Square, accum_out=ssq[:, tt:tt + 1]).then_inc(x_ss, 1)
                act.wait_ge(x_ss, 2 * tt + 1)
                A(rst[:, tt:tt + 1], ssq[:, tt:tt + 1], ACT.Ln, scale=1.0 / D, bias=EPSB).then_inc(x_ss, 1)
                act.wait_ge(x_ss, 2 * tt + 2)
                A(rst[:, tt:tt + 1], rst[:, tt:tt + 1], ACT.Exp, scale=-0.5).then_inc(x_rst, 1)

            def x_hi_part(tt):
                act.wait_ge(x_tr, tt + 1)
                A(h_hi[:, :].rearrange("p (k t) -> p k t", t=T)[:, :, tt * P:(tt + 1) * P],
                  bank(4 * (tt % 2), 4).rearrange("p (k t) -> p k t", t=P), ACT.Copy).then_inc(x_hi, 1)

            act.wait_ge(eps_ready, 1)
            x_stats(0)
            x_stats(1)
            x_hi_part(0)
            x_stats(2)
            x_hi_part(1)
            x_stats(3)
            act.wait_ge(lb_v, 1)
            A(lbw[:, 0:H], lbw[:, 0:H], ACT.Exp).then_inc(lb_s, 1)
            x_hi_part(2)
            hi_unit(0, 0, 0, first=True)
            x_hi_part(3)
            hi_unit(1, 1, 0, first=True)
            act.wait_ge(lb_v, 5)
            A(lbp[:, 0:H], lbw[:, H:2 * H], ACT.Ln, scale=-1.0, bias=1.0).then_inc(lb_s, 1)
            A(lbw[:, 3 * H:4 * H], lbw[:, 2 * H:3 * H], ACT.Ln).then_inc(lb_s, 1)

            def take_gb(j):
                act.wait_ge(unit_done, CONV_U * (j + 1))
                A(gates[:, ds(j * T, T)], bank(gb_bank[0]), ACT.Copy).then_inc(gb_taken, 1)

            def conv_channel(j, r, q0, first, start):
                for s in range(CONV_U):
                    m = CONV_U * r + s + AHEAD
                    hi_unit(CONV_U * j + s + AHEAD, m % RING, q0 + m // RING, start and m < RING)
                    if s == 0 and not first:
                        gb_bank[0] = (3 * (r + 1) + 2) % 2
                        take_gb(j - 1)
                    if s == 2:
                        act.wait_ge(unit_done, CONV_U * j + 2)
                        if not first:
                            act.wait_ge(u_taken, j)
                        softplus_of_abs(bank((3 * r) % 2), glu, ug_s, 3 * j)
                    if s == 3:
                        act.wait_ge(ug_taken, j + 1)
                        A(glu, glu, ACT.Exp).then_inc(glu_ready, 1)

            gb_bank = [0]
            conv_channel(0, 0, 0, True, True)
            conv_channel(1, 1, 0, False, False)
            with act.Fori(1, J // 2) as i:
                conv_channel(2 * i, 0, 3 * i, False, False)
                conv_channel(2 * i + 1, 1, 3 * i, False, False)

            def ln_square(j):
                act.wait_ge(cen_done, J)
                if j >= 2:
                    act.wait_ge(vacc_done, j - 1)
                A((t1, t2)[j % 2], mix[:, (H + j) * T:(H + j + 1) * T], ACT.Square).then_inc(csq_done, 1)

            def ln_rstd():
                act.wait_ge(var_done, 1)
                A(lnr, bank(3), ACT.Ln, scale=1.0 / W_B, bias=EPSB).then_inc(lnr_s, 1)
                act.wait_ge(lnr_s, 1)
                A(lnr, lnr, ACT.Exp, scale=-0.5).then_inc(lnr_s, 1)

            def ln_tile(j, s):
                if s == 0:
                    act.wait_ge(ln_v, 7 * j + 2)
                    A(t3, t1, ACT.Abs).then_inc(ln_s, 1)
                    A(t4, gates[:, ds(j * T, T)], ACT.Abs).then_inc(ln_s, 1)
                    act.wait_ge(ln_s, 4 * j + 2)
                    A(part(2, 2), part(2, 2), ACT.Exp, scale=-1.0).then_inc(ln_s, 1)
                    act.wait_ge(ln_s, 4 * j + 3)
                    A(part(2, 2), part(2, 2), ACT.Ln, bias=1.0).then_inc(ln_s, 1)
                if s == 1:
                    act.wait_ge(ln_v, 7 * j + 5)
                    A(t3, t3, ACT.Exp).then_inc(ln_sig, 1)

            def own(h, u, first):
                base = N_HEAD + HEAD_U * h
                if u == 2:
                    act.wait_ge(unit_done, base + 2)
                    if not first:
                        act.wait_ge(head_done, h - 1) if not isinstance(h, int) or h > 1 else None
                    softplus_of_abs(bank(0), t1, f_s, 3 * h)
                if u == 3:
                    act.wait_ge(f_v, 8 * h + 2)
                    if not first:
                        act.wait_ge(lev_done, 4 * h - 3)
                        act.wait_ge(kdec_ready, h)
                        act.wait_ge(qdec_ready, h)
                    A(key, t3, ACT.Exp, scale=-1.0, bias=hcur[:, 0:1]).then_inc(key_ready, 1)
                    A(t1, t2, ACT.Abs, bias=hcur[:, 2:3]).then_inc(f_la, 1)
                    act.wait_ge(f_la, 3 * h + 1)
                    A(t1, t1, ACT.Exp, scale=-1.0).then_inc(f_la, 1)
                    act.wait_ge(f_la, 3 * h + 2)
                    A(t1, t1, ACT.Ln, bias=1.0).then_inc(f_la, 1)
                if u == 4:
                    act.wait_ge(unit_done, base + 4)
                    if not first:
                        act.wait_ge(lev_done, 4 * h - 3)
                    A(qry, bank(1), ACT.Copy, scale=Q_SCALE).then_inc(q_taken, 1)
                    for n in range(4):
                        act.wait_ge(lev_d, 7 * h + n + 1)
                        A(lev[n], lev[n], ACT.Exp).then_inc(lev_e, 1)
                if u == 5:
                    for n in (4, 5):
                        act.wait_ge(lev_d, 7 * h + n + 1)
                        A(lev[n], lev[n], ACT.Exp).then_inc(lev_e, 1)
                    act.wait_ge(lev_d, 7 * h + 7)
                    A(cut(kmod, 1, 0), cut(kmod, 1, 0), ACT.Exp).then_inc(lev_e, 1)
                    A(cut(kmod, 1, 1), cut(key, 1, 1), ACT.Copy).then_inc(lev_e, 1)
                    if not first:
                        act.wait_ge(st_done, h)
                        act.wait_ge(st_v, 3 * h)
                    for c in range(TT - 1):
                        A(kdec[:, c * P:(c + 1) * P], bcum[:, c * P:(c + 1) * P], ACT.Exp, scale=-1.0,
                          bias=bcum[:, (c + 1) * P - 1:(c + 1) * P]).then_inc(kdec_e, 1)
                    A(ebl[:, 0:TT - 1], bcum.rearrange("p (c t) -> p c t", t=P)[:, 0:TT - 1, P - 1], ACT.Exp).then_inc(ebl_ready, 1)
                if u == 6:
                    if not first:
                        act.wait_ge(o_done, h)
                    A(qdec[:, P:T], bcum[:, P:T], ACT.Exp).then_inc(qdec_e, 1)
                    act.wait_ge(unit_done, base + 6)
                    A(vals, bank(0), ACT.Copy).then_inc(v_taken, 1)

            def late(g, u, first):
                if u == 0:
                    act.wait_ge(unit_done, N_HEAD + HEAD_U * (g + 1))
                    if not first:
                        act.wait_ge(head_done, g)
                    A(sgate, bank(1), ACT.Copy).then_inc(gate_taken, 1)
                    act.wait_ge(gate_taken, g + 1)
                    softplus_of_abs(sgate, t4, gate_s, 3 * g)
                if u == 1:
                    act.wait_ge(vt_done, g + 1)
                    A(vals, XB, ACT.Copy).then_inc(vt_taken, 1)
                    act.wait_ge(gate_ls, g + 1)
                    A(t4, t4, ACT.Exp).then_inc(gate_sig, 1)
                if u == 2:
                    act.wait_ge(kt_done, g + 1)
                    A(kdec[:, 0:T - P], XB[:, 0:T - P], ACT.Copy).then_inc(kt_taken, 1)
                if u == 6:
                    act.wait_ge(o_done, g + 1)
                    act.wait_ge(gate_ready, g + 1)
                    act.wait_ge(ln_v, 7 * g + 6)
                    A(t4, OB, ACT.Square).then_inc(osq_done, 1)
                if u == 7:
                    act.wait_ge(norm_done, g + 1)
                    A(t1, XB, ACT.Ln, scale=1.0 / P, bias=EPSB).then_inc(rs_s, 1)
                    act.wait_ge(rs_s, 2 * g + 1)
                    A(t1, t1, ACT.Exp, scale=-0.5).then_inc(rs_s, 1)

            def head_step(h, u, q0):
                base = N_HEAD + HEAD_U * h
                hi_unit(base + u + AHEAD, (u + AHEAD) % RING, q0 + (u + AHEAD) // RING)

            for u in range(HEAD_U):
                head_step(0, u, N_HEAD // RING)
                if u == 0:
                    gb_bank[0] = 1
                    take_gb(J - 1)
                own(0, u, True)
                if u >= 6:
                    for j in range(J // 2 * (u - 6), J // 2 * (u - 5)):
                        ln_square(j)

            def head_rest(h, first):
                for u in range(HEAD_U):
                    head_step(h, u, N_HEAD // RING + 2 * h)
                    if first and u == 0:
                        ln_rstd()
                    late(h - 1, u, first)
                    own(h, u, False)
                    if u in (4, 5):
                        ln_tile(h - 1, u - 4)

            head_rest(1, True)
            with act.Fori(2, H) as h:
                head_rest(h, False)

            def mix_hi(at):
                m = MIX_AT[at]
                act.wait_ge(unit_done, N_OUT - 1 if at < HK else N_OUT)
                if m < H:
                    act.wait_ge(head_done, m + 1)
                else:
                    act.wait_ge(ln_v, 7 * (m - H + 1))
                A(h_hi[:, at * T:(at + 1) * T], mix[:, m * T:(m + 1) * T], ACT.Copy).then_inc(mhi_done, 1)

            def take_sq(c, tt):
                act.wait_ge(y_taken, TT * c + tt + 1)
                if c:
                    act.wait_ge(y_sq, TT * (c - 1) + tt + 1)
                A(part(tt), bank(4 * (c % 2) + tt), ACT.Square, accum_out=ssq[:, tt * CHUNKS + c:tt * CHUNKS + c + 1]).then_inc(y_sq, 1)

            def out_hi(c, s):
                n = N_OUT + OUT_U * c + s + AHEAD
                if n < N_END:
                    hi_unit(n, n % RING, n // RING)

            for at in range(6):
                mix_hi(at)
            for s in range(OUT_U):
                out_hi(0, s)
                late(H - 1, s, False)
                if s in (2, 3):
                    ln_tile(J - 1, s - 2)
                for at in {0: (6, 7), 1: (8, 9), 2: (10, 11), 3: (12,), 5: (13, 14), 7: (15,)}.get(s, ()):
                    mix_hi(at)
                if s == 5:
                    act.dma_start(gates[:, 0:D], post_norm_g[0].partition_broadcast(P)).then_inc(gain_in, 16)
            for c in range(1, CHUNKS):
                for s in range(OUT_U):
                    out_hi(c, s)
                    if c == 1 and s == 0:
                        act.wait_ge(mlo_done, KT)
                        for tt in range(TT):
                            act.dma_start(work[:, 4 * T + tt * D:4 * T + (tt + 1) * D], x[0, tt * P:(tt + 1) * P, :]).then_inc(res_in, 16)
                    if s in (1, 2):
                        take_sq(c - 1, 2 * s - 2)
                        take_sq(c - 1, 2 * s - 1)
            for tt in range(TT):
                take_sq(CHUNKS - 1, tt)
                act.wait_ge(y_ssum, tt + 1)
                A(rst[:, tt:tt + 1], rst[:, TT + tt:TT + tt + 1], ACT.Ln, scale=1.0 / D, bias=EPSB).then_inc(y_rs, 1)
                act.wait_ge(y_rs, 2 * tt + 1)
                A(rst[:, tt:tt + 1], rst[:, tt:tt + 1], ACT.Exp, scale=-0.5).then_inc(y_rs, 1)

        @block.vector
        def _(dve):
            V = nc.vector
            V.memset(epsb[:], EPS).then_inc(eps_ready, 1)
            V.memset(apad[0][:, 0:TAPS - 1], 0.0)
            V.memset(apad[1][:, 0:TAPS - 1], 0.0)

            def x_scale(tt):
                dve.wait_ge(x_rst, tt + 1)
                if tt == 0:
                    dve.wait_ge(gain_in, 16)
                a = mix[:, tt * D:(tt + 1) * D]
                V.scalar_tensor_tensor(a, a, rst[:, tt:tt + 1], gates[:, 0:D], ALU.mult, ALU.mult).then_inc(x_norm, 1)

            def x_lo_part(tt):
                dve.wait_ge(x_hi, tt + 1)
                v = slice(tt * P, (tt + 1) * P)
                V.tensor_tensor(h_lo[:, :].rearrange("p (k t) -> p k t", t=T)[:, :, v],
                                bank(4 * (tt % 2), 4).rearrange("p (k t) -> p k t", t=P),
                                h_hi[:, :].rearrange("p (k t) -> p k t", t=T)[:, :, v].bitcast(fp32),
                                ALU.subtract).then_inc(x_lo, 1)

            dve.wait_ge(par_t, 1)
            V.tensor_copy(par[:, :], bank(0)[:, 0:NPAR * J + 1]).then_inc(par_ready, 1)
            dve.wait_ge(par_ready, 1)
            lgt = par3[:, TAPS + 3, :]
            V.tensor_tensor(lbw[:, 0:H], lgt, lgt, ALU.subtract).then_inc(lb_v, 1)
            x_scale(0)
            x_scale(1)
            x_lo_part(0)
            x_scale(2)
            x_lo_part(1)
            x_scale(3)
            dve.wait_ge(lb_s, 1)
            V.reciprocal(lbw[:, H:2 * H], lbw[:, 0:H]).then_inc(lb_v, 1)
            dve.wait_ge(lb_v, 2)
            V.tensor_tensor(lbw[:, 0:H], lbw[:, 0:H], lbw[:, H:2 * H], ALU.mult).then_inc(lb_v, 1)
            dve.wait_ge(lb_v, 3)
            V.tensor_tensor(lbw[:, H:2 * H], lbw[:, 0:H], lbw[:, 0:H], ALU.subtract).then_inc(lb_v, 1)
            dve.wait_ge(lb_v, 4)
            V.tensor_scalar(lbw[:, 2 * H:3 * H], lbw[:, H:2 * H], LB_FLOOR, 2.0 ** 50, ALU.max, ALU.mult).then_inc(lb_v, 1)
            x_lo_part(2)
            x_lo_part(3)
            dve.wait_ge(lb_s, 3)
            V.tensor_scalar(lbp[:, H:2 * H], lbw[:, 3 * H:4 * H], LN2_50, None, ALU.subtract).then_inc(lb_v, 1)
            dve.wait_ge(lb_v, 6)
            V.tensor_tensor(lbp[:, 2 * H:3 * H], lbp[:, 0:H], lbp[:, H:2 * H], ALU.subtract).then_inc(lb_v, 1)

            def conv_taps(j, r, a, b):
                acc = bank(2 + r)
                tp = tap[:, r * (TAPS + 1):(r + 1) * (TAPS + 1)]
                for w in range(a, b):
                    src = apad[r][:, w:w + T]
                    if w == 0:
                        V.tensor_scalar(acc, src, tp[:, 0:1], tp[:, TAPS:TAPS + 1], ALU.mult, ALU.add).then_inc(tap_done, 1)
                    else:
                        dve.wait_ge(tap_done, TAPS * j + w)
                        dst = acc if w < TAPS - 1 else mix[:, ds((H + j) * T, T)]
                        V.scalar_tensor_tensor(dst, src, tp[:, w:w + 1], acc, ALU.mult, ALU.add).then_inc(tap_done, 1)

            def add_to_sum(j, first):
                dve.wait_ge(tap_done, TAPS * (j + 1))
                y = mix[:, ds((H + j) * T, T)]
                if first:
                    V.tensor_copy(lnr, y).then_inc(ysum_done, 1)
                else:
                    dve.wait_ge(ysum_done, j)
                    V.tensor_tensor(lnr, lnr, y, ALU.add).then_inc(ysum_done, 1)

            def finish_conv(j, r, s, first):
                a, b = ((11, 17), (17, 23), (23, 27), (27, TAPS))[s]
                conv_taps(j, r, a, b)
                if s == 3:
                    add_to_sum(j, first)

            def conv_channel(j, r, first, second):
                for s in range(CONV_U):
                    if s == 2:
                        dve.wait_ge(ug_s, 3 * (j + 1))
                        V.scalar_tensor_tensor(glu, bank((3 * r) % 2), 0.0, glu, ALU.min, ALU.subtract).then_inc(ug_taken, 1)
                    if s < 4 and not first:
                        finish_conv(j - 1, 1 - r, s, second)
                    if s == 4:
                        dve.wait_ge(glu_ready, j + 1)
                        dve.wait_ge(unit_done, CONV_U * j + 4)
                        V.tensor_tensor(apad[r][:, TAPS - 1:], bank((3 * r + 1) % 2), glu, ALU.mult).then_inc(u_taken, 1)
                        V.tensor_copy(tap[:, r * (TAPS + 1):(r + 1) * (TAPS + 1)], par3[:, 0:TAPS + 1, j]).then_inc(tap_ready, 1)
                        dve.wait_ge(u_taken, j + 1)
                        dve.wait_ge(tap_ready, j + 1)
                        conv_taps(j, r, 0, 5)
                    if s == 5:
                        conv_taps(j, r, 5, 11)

            conv_channel(0, 0, True, False)
            conv_channel(1, 1, False, True)
            with dve.Fori(1, J // 2) as i:
                conv_channel(2 * i, 0, False, False)
                conv_channel(2 * i + 1, 1, False, False)

            def centre():
                dve.wait_ge(mean_done, 1)
                for j in range(J):
                    y = mix[:, (H + j) * T:(H + j + 1) * T]
                    V.scalar_tensor_tensor(y, bank(2), -1.0 / W_B, y, ALU.mult, ALU.add).then_inc(cen_done, 1)

            def add_squares(j0, j1):
                for j in range(j0, j1):
                    dve.wait_ge(csq_done, j + 1)
                    sq = (t1, t2)[j % 2]
                    if j:
                        dve.wait_ge(vacc_done, j)
                        V.tensor_tensor(t3, t3, sq, ALU.add).then_inc(vacc_done, 1)
                    else:
                        V.tensor_copy(t3, sq).then_inc(vacc_done, 1)

            def ln_tile(j, s, first):
                y = mix[:, ds((H + j) * T, T)]
                gb = gates[:, ds(j * T, T)]
                if s == 0:
                    if first:
                        dve.wait_ge(lnr_s, 2)
                    V.tensor_copy(lnp[:, :], par3[:, TAPS + 1:TAPS + 3, j]).then_inc(ln_v, 1)
                    V.tensor_tensor(t1, y, lnr, ALU.mult).then_inc(ln_x, 1)
                    dve.wait_ge(ln_v, 7 * j + 1)
                    dve.wait_ge(ln_x, j + 1)
                    V.tensor_scalar(t1, t1, lnp[:, 0:1], lnp[:, 1:2], ALU.mult, ALU.add).then_inc(ln_v, 1)
                if s == 1:
                    dve.wait_ge(ln_s, 4 * (j + 1))
                    V.scalar_tensor_tensor(t3, t1, 0.0, t3, ALU.min, ALU.subtract).then_inc(ln_v, 1)
                    V.scalar_tensor_tensor(t4, gb, 0.0, t4, ALU.min, ALU.subtract).then_inc(ln_v, 1)
                    dve.wait_ge(ln_v, 7 * j + 4)
                    V.tensor_tensor(t3, t3, t4, ALU.add).then_inc(ln_v, 1)
                    V.tensor_tensor(t2, t1, gb, ALU.mult).then_inc(ln_v, 1)
                if s == 2:
                    dve.wait_ge(ln_sig, j + 1)
                    dve.wait_ge(ln_v, 7 * j + 6)
                    V.tensor_tensor(y, t2, t3, ALU.mult).then_inc(ln_v, 1)

            def own(h, u, first):
                base = N_HEAD + HEAD_U * h
                if u == 2:
                    if not first:
                        dve.wait_ge(f_la, 3 * h)
                    V.tensor_copy(hcur[:, :], lbp[:, :].rearrange("p (n j) -> p n j", j=H)[:, :, h]).then_inc(hc_ready, 1)
                    dve.wait_ge(f_s, 3 * (h + 1))
                    V.scalar_tensor_tensor(t2, bank(0), 0.0, t1, ALU.min, ALU.subtract).then_inc(f_v, 1)
                    V.scalar_tensor_tensor(t3, bank(0), 0.0, t1, ALU.max, ALU.add).then_inc(f_v, 1)
                if u == 3:
                    dve.wait_ge(f_la, 3 * h + 1)
                    dve.wait_ge(hc_ready, h + 1)
                    V.tensor_scalar(t2, t2, hcur[:, 0:1], hcur[:, 1:2], ALU.add, ALU.max).then_inc(f_v, 1)
                    dve.wait_ge(f_la, 3 * h + 3)
                    dve.wait_ge(f_v, 8 * h + 3)
                    V.tensor_tensor(t2, t2, t1, ALU.add).then_inc(f_v, 1)
                    dve.wait_ge(f_v, 8 * h + 4)
                    if not first:
                        dve.wait_ge(qdec_e, h)
                    for c in range(TT):
                        v = slice(c * P, (c + 1) * P)
                        V.tensor_tensor_scan(bcum[:, v], ones[:, :], t2[:, v], 0.0, ALU.mult, ALU.add).then_inc(f_v, 1)
                    dve.wait_ge(f_v, 8 * h + 8)
                    level_diffs(0, 4)
                if u == 4:
                    level_diffs(4, 6)
                    V.tensor_tensor(cut(kmod, 1, 0), cut(bcum, 1, 1), cut(bcum, 1, 0), ALU.subtract).then_inc(lev_d, 1)
                    dve.wait_ge(key_ready, h + 1)
                    level_times(h, 0, 4, 0, key)
                if u == 5:
                    dve.wait_ge(q_taken, h + 1)
                    level_times(h, 0, 4, 1, qry)
                if u == 6:
                    level_times(h, 4, 6, 0, key)
                    level_times(h, 4, 6, 1, qry)
                    dve.wait_ge(lev_e, 8 * h + 8)
                    V.tensor_tensor(cut(kmod, 1, 0), cut(kmod, 1, 0), cut(key, 1, 0), ALU.mult).then_inc(lev_ready, 1)
                    dve.wait_ge(kdec_e, 3 * (h + 1))
                    V.tensor_tensor(kdec[:, 0:T - P], kdec[:, 0:T - P], key[:, 0:T - P], ALU.mult).then_inc(kdec_ready, 1)
                if u == 7:
                    dve.wait_ge(qdec_e, h + 1)
                    V.tensor_tensor(qdec[:, P:T], qdec[:, P:T], qry[:, P:T], ALU.mult).then_inc(qdec_ready, 1)

            def level_diffs(a, b):
                for n in range(a, b):
                    m = LEVELS[n]
                    even, odd = cut(bcum, m, 0), cut(bcum, m, 1)
                    ref = even[:, :, m - 1:m].broadcast_to([P, T // (2 * m), m])
                    V.tensor_tensor(cut(lev[n], m, 0), ref, even, ALU.subtract)
                    V.tensor_tensor(cut(lev[n], m, 1), odd, ref, ALU.subtract).then_inc(lev_d, 1)

            def level_times(h, a, b, odd, what):
                for n in range(a, b):
                    m = LEVELS[n]
                    dve.wait_ge(lev_e, 8 * h + n + 1)
                    V.tensor_tensor(cut(lev[n], m, odd), cut(lev[n], m, odd), cut(what, m, odd), ALU.mult)

            def take_scores(g, k, src):
                n = (NL + k) % (NL + 2)
                m = (LEVELS + [1, 1])[n]
                if k:
                    copied = held(dve, (NL + 2) * g + k)
                    dve.wait_ge(masks_ready, 1)
                    dve.wait_ge(probs_done, copied)
                V.copy_predicated(cut(probs, m, 1 if n <= NL else 0), runs(mask[:, n * HALF:(n + 1) * HALF], m),
                                  runs(src[:, 0:HALF], m)).then_inc(probs_done, 1)

            def late(g, u, first):
                if u == 1:
                    dve.wait_ge(gate_s, 3 * (g + 1))
                    V.scalar_tensor_tensor(t4, sgate, 0.0, t4, ALU.min, ALU.subtract).then_inc(gate_ls, 1)
                if u == 2:
                    dve.wait_ge(gate_sig, g + 1)
                    V.tensor_tensor(sgate, sgate, t4, ALU.mult).then_inc(gate_ready, 1)
                if 1 <= u <= 4:
                    scored = held(dve, 4 * g + u)
                    used = held(dve, g)
                    dve.wait_ge(masks_ready, 1)
                    dve.wait_ge(lev_done, scored)
                    if u == 1 and not first:
                        dve.wait_ge(o_done, used)
                    take_scores(g, 2 * u - 2, LV0)
                    take_scores(g, 2 * u - 1, LV1)
                if u == 4:
                    dve.wait_ge(st_done, g + 1)
                    if not first:
                        dve.wait_ge(o_done, g)
                    V.tensor_copy(state[:, 0:P], XB[:, 0:P]).then_inc(st_v, 1)
                    dve.wait_ge(ebl_ready, g + 1)
                    for c in range(1, TT - 1):
                        dve.wait_ge(st_v, (TT - 1) * g + c)
                        V.scalar_tensor_tensor(state[:, c * P:(c + 1) * P], state[:, (c - 1) * P:c * P], ebl[:, c:c + 1],
                                               XB[:, c * P:(c + 1) * P], ALU.mult, ALU.add).then_inc(st_v, 1)
                if u == 7:
                    dve.wait_ge(rs_s, 2 * (g + 1))
                    V.tensor_tensor(t1, OB, t1, ALU.mult).then_inc(on_done, 1)
                    dve.wait_ge(on_done, g + 1)
                    dve.wait_ge(gate_ready, g + 1)
                    V.scalar_tensor_tensor(mix[:, ds(g * T, T)], t1, par[:, HGC:HGC + 1], sgate, ALU.mult, ALU.mult).then_inc(head_done, 1)

            for u in range(HEAD_U):
                if u < 4:
                    finish_conv(J - 1, 1, u, False)
                own(0, u, True)
                if u == 5:
                    centre()
                if u >= 6:
                    add_squares(J // 2 * (u - 6), J // 2 * (u - 5))

            dve.wait_ge(masks_ready, 1)

            def head_rest(h, first):
                for u in range(HEAD_U):
                    late(h - 1, u, first)
                    if u in (4, 5, 6):
                        ln_tile(h - 1, u - 4, first)
                    own(h, u, False)

            head_rest(1, True)
            with dve.Fori(2, H) as h:
                head_rest(h, False)

            def mix_lo(at):
                m = MIX_AT[at]
                dve.wait_ge(mhi_done, at + 1)
                a = slice(at * T, (at + 1) * T)
                V.tensor_tensor(h_lo[:, a], mix[:, m * T:(m + 1) * T], h_hi[:, a].bitcast(fp32), ALU.subtract).then_inc(mlo_done, 1)

            def take_y(c, tt):
                if tt < TT - 1:
                    dve.wait_ge(y_mm, (TT - 1) * c + tt + 1)
                else:
                    dve.wait_ge(unit_done, N_OUT + OUT_U * (c + 1))
                V.tensor_tensor(mix[:, tt * D + c * 512:tt * D + (c + 1) * 512], bank(4 * (c % 2) + tt),
                                gates[:, c * 512:(c + 1) * 512], ALU.mult).then_inc(y_taken, 1)

            for at in range(6):
                mix_lo(at)
            for s in range(OUT_U):
                late(H - 1, s, False)
                if s in (2, 3, 4):
                    ln_tile(J - 1, s - 2, False)
                for at in {0: (6, 7), 1: (8, 9), 2: (10, 11), 3: (12,), 5: (13, 14), 7: (15,)}.get(s, ()):
                    mix_lo(at)
            dve.wait_ge(gain_in, 32)
            for c in range(CHUNKS - 1):
                for tt in range(TT):
                    take_y(c, tt)
            dve.wait_ge(res_in, 16 * TT)
            for tt in range(TT):
                take_y(CHUNKS - 1, tt)
                dve.wait_ge(y_sq, TT * (CHUNKS - 1) + tt + 1)
                V.tensor_reduce(rst[:, TT + tt:TT + tt + 1], ssq[:, tt * CHUNKS:(tt + 1) * CHUNKS], AX.X, ALU.add).then_inc(y_ssum, 1)
                dve.wait_ge(y_rs, 2 * (tt + 1))
                dve.wait_ge(y_taken, TT * (CHUNKS - 1) + tt + 1)
                a = mix[:, tt * D:(tt + 1) * D]
                V.scalar_tensor_tensor(a, a, rst[:, tt:tt + 1], work[:, 4 * T + tt * D:4 * T + (tt + 1) * D],
                                       ALU.mult, ALU.add).then_inc(y_out, 1)

        @block.tensor
        def _(pe):
            mm = nc.tensor.matmul

            pe.wait_ge(masks_ready, 1)
            pe.wait_ge(par_in, 16 * 7)
            last = 3 * J + 1
            nc.tensor.transpose(bank(0)[:, 0:P], stage[:, 0:P], ident[:, :])
            nc.tensor.transpose(bank(0)[:, P:2 * P], stage[:, P:2 * P], ident[:, :])
            nc.tensor.transpose(bank(0)[:, 2 * P:2 * P + last], stage[0:last, 2 * P:3 * P], ident[0:last, 0:last]).then_inc(par_t, 1)

            for tt in range(TT):
                pe.wait_ge(x_norm, tt + 1)
                if tt == 0:
                    pe.wait_ge(par_ready, 1)
                if tt >= 2:
                    pe.wait_ge(x_lo, tt - 1)
                for k in range(KT):
                    ins = nc.tensor.transpose(bank(4 * (tt % 2), 4)[:, k * P:(k + 1) * P],
                                              mix[:, tt * D + k * P:tt * D + (k + 1) * P], ident[:, :])
                ins.then_inc(x_tr, 1)

            def project(n, slot, half, b):
                pe.wait_ge(lo_done, n + 1)
                for k in range(HK):
                    kt = half * HK + k
                    wh = w_hi[:, slot * UW + k * P:slot * UW + (k + 1) * P]
                    wl = w_lo[:, slot * UW + k * P:slot * UW + (k + 1) * P]
                    hh, hl = h_hi[:, kt * T:(kt + 1) * T], h_lo[:, kt * T:(kt + 1) * T]
                    mm(bank(b), wh, hh, start=kt == 0, stop=False)
                    mm(bank(b), wh, hl, start=False, stop=False)
                    ins = mm(bank(b), wl, hh, start=False, stop=kt == KT - 1)
                ins.then_inc(unit_done, 1)

            def conv_channel(j, r, first):
                for s in range(CONV_U):
                    if s == 0 and not first:
                        pe.wait_ge(u_taken, j)
                    if s == 2 and not first:
                        pe.wait_ge(gb_taken, j)
                    if s == 4:
                        pe.wait_ge(ug_taken, j + 1)
                    project(CONV_U * j + s, (CONV_U * r + s) % RING, s % 2, (3 * r + s // 2) % 2)

            pe.wait_ge(x_lo, TT)
            conv_channel(0, 0, True)
            conv_channel(1, 1, False)
            with pe.Fori(1, J // 2) as i:
                conv_channel(2 * i, 0, False)
                conv_channel(2 * i + 1, 1, False)

            def slot(g, u, first):
                if u == 0:
                    pe.wait_ge(lev_ready, g + 1)
                    if not first:
                        pe.wait_ge(probs_done, 8 * g)
                    for c in range(TT):
                        kb, qb = slice(c * P, (c + 1) * P), slice(c * P // 2, (c + 1) * P // 2)
                        mm(LV0[:, qb], kmod[:, kb], cut(qry[:, kb], 1, 1)[:, :, 0], start=True, stop=True)
                        ins = mm(LV1[:, qb], key[:, kb], cut(qry[:, kb], 1, 0)[:, :, 0], start=True, stop=True)
                    ins.then_inc(lev_done, 1)
                    pe.wait_ge(v_taken, g + 1)
                    if not first:
                        pe.wait_ge(rs_s, 2 * g)
                    for c in range(TT):
                        ins = nc.tensor.transpose(XB[:, c * P:(c + 1) * P], vals[:, c * P:(c + 1) * P], ident[:, :])
                    ins.then_inc(vt_done, 1)
                if 1 <= u <= 3:
                    pe.wait_ge(probs_done, 8 * g + 2 * u)
                    for n in (2 * u - 2, 2 * u - 1):
                        m = LEVELS[n]
                        for c in range(TT):
                            kb, qb = slice(c * P, (c + 1) * P), slice(c * P // 2, (c + 1) * P // 2)
                            ins = mm((LV0, LV1)[n % 2][:, qb].rearrange("p (g m) -> p g m", m=m),
                                     lev[n][:, kb], cut(lev[n][:, kb], m, 1), start=True, stop=True)
                    ins.then_inc(lev_done, 1)
                if u == 1:
                    pe.wait_ge(vt_taken, g + 1)
                    pe.wait_ge(kdec_ready, g + 1)
                    for c in range(TT - 1):
                        ins = nc.tensor.transpose(XB[:, c * P:(c + 1) * P], kdec[:, c * P:(c + 1) * P], ident[:, :])
                    ins.then_inc(kt_done, 1)
                if u == 3:
                    pe.wait_ge(kt_taken, g + 1)
                    for c in range(TT - 1):
                        v = slice(c * P, (c + 1) * P)
                        ins = mm(XB[:, v], kdec[:, v], vals[:, v], start=True, stop=True)
                    ins.then_inc(st_done, 1)
                if u == 5:
                    pe.wait_ge(probs_done, 8 * (g + 1))
                    pe.wait_ge(st_v, (TT - 1) * (g + 1))
                    pe.wait_ge(qdec_ready, g + 1)
                    if not first:
                        pe.wait_ge(head_done, g)
                    for c in range(TT):
                        v = slice(c * P, (c + 1) * P)
                        ins = mm(OB[:, v], vals[:, v], probs[:, v], start=True, stop=c == 0)
                        if c:
                            ins = mm(OB[:, v], state[:, (c - 1) * P:c * P], qdec[:, v], start=False, stop=True)
                    ins.then_inc(o_done, 1)
                if u == 6:
                    pe.wait_ge(osq_done, g + 1)
                    mm(XB, ones[:, :], t4, start=True, stop=True).then_inc(norm_done, 1)

            def head(h, first, second):
                for u in range(HEAD_U):
                    if u == 0:
                        pe.wait_ge(u_taken, J) if first else pe.wait_ge(v_taken, h)
                    if u == 2:
                        pe.wait_ge(gb_taken, J) if first else pe.wait_ge(gate_taken, h)
                    if u == 4:
                        pe.wait_ge(f_v, 8 * h + 2)
                    if u == 6:
                        pe.wait_ge(q_taken, h + 1)
                    project(N_HEAD + HEAD_U * h + u, u % RING, u % 2, (u // 2) % 2)
                    if not first:
                        slot(h - 1, u, second)
                    if first and u == 4:
                        pe.wait_ge(ysum_done, J)
                        mm(bank(2), ones[:, :], lnr, start=True, stop=True).then_inc(mean_done, 1)
                    if first and u == HEAD_U - 1:
                        pe.wait_ge(vacc_done, J)
                        mm(bank(3), ones[:, :], t3, start=True, stop=True).then_inc(var_done, 1)

            head(0, True, False)
            head(1, False, True)
            with pe.Fori(2, H) as h:
                head(h, False, False)

            for c in range(CHUNKS):
                for s in range(OUT_U):
                    if c == 0:
                        slot(H - 1, s, False)
                    if c == 0 and s == 0:
                        pe.wait_ge(gate_taken, H)
                    if s == 0 and c >= 2:
                        pe.wait_ge(y_sq, TT * (c - 1))
                    n = N_OUT + OUT_U * c + s
                    pe.wait_ge(lo_done, n + 1)
                    if c == 0:
                        pe.wait_ge(mlo_done, 2 * s + 2)
                    for tt in range(TT):
                        for k in range(2):
                            a = slice((2 * s + k) * T + tt * P, (2 * s + k) * T + (tt + 1) * P)
                            w = slice((s % RING) * UW + k * 512, (s % RING) * UW + (k + 1) * 512)
                            o = bank(4 * (c % 2) + tt)
                            mm(o, h_hi[:, a], w_hi[:, w], start=s == 0 and k == 0, stop=False)
                            mm(o, h_hi[:, a], w_lo[:, w], start=False, stop=False)
                            ins = mm(o, h_lo[:, a], w_hi[:, w], start=False, stop=s == OUT_U - 1 and k == 1)
                        if s == OUT_U - 1 and tt < TT - 1:
                            ins.then_inc(y_mm, 1)
                    ins.then_inc(unit_done, 1)


_INS = ["x", "pre_norm_g", "post_norm_g", "w_in", "lb_logits", "hg_norm_g", "dw_kernel", "dw_bias",
        "conv_ln_g", "conv_ln_b", "w_out"]


def kernel(**inputs):
    import numpy as np
    import concourse.bacc as bacc
    from concourse.bass_utils import run_bass_kernel_spmd

    nc = bacc.Bacc("TRN2", target_bir_lowering=False, num_devices=1)
    arrays, args = {}, []
    for name in _INS:
        a = np.ascontiguousarray(inputs[name])
        arrays[f"in_{name}"] = a
        args.append(nc.dram_tensor(f"in_{name}", a.shape, mybir.dt.from_np(a.dtype), kind="ExternalInput").ap())
    shape = inputs["x"].shape
    args.append(nc.dram_tensor("out_y", shape, mybir.dt.float32, kind="ExternalOutput").ap())
    build_layer(nc, *args)
    r = run_bass_kernel_spmd(nc, [arrays], core_ids=[0])
    return r.results[0]["out_y"]
```

```python
from contextlib import ExitStack

import concourse.bass as bass
from concourse import mybir


def build_layer(nc, x, pre_norm_g, post_norm_g, w_in, lb_logits, hg_norm_g, dw_kernel, dw_bias,
                conv_ln_g, conv_ln_b, w_out, out):
    fp32, fp32r, i8 = mybir.dt.float32, mybir.dt.float32r, mybir.dt.int8
    ALU, ACT, AX = mybir.AluOpType, mybir.ActivationFunctionType, mybir.AxisListType
    ds = bass.ds
    P = 128
    _, T, D = x.shape
    W_A = lb_logits.shape[1]
    W_B = dw_bias.shape[1]
    TAPS = dw_kernel.shape[1]
    H = W_A // P
    J = W_B // P
    KT = D // P
    HK = KT // 2
    TT = T // P
    UW = HK * P
    RING = 4
    EPS, LB_FLOOR = 1e-6, 1e-30
    Q_SCALE = float(P) ** -0.5
    LN2_50 = 34.657359027997264
    AHEAD = 2

    CONV_T, HEAD_T = 3, 4
    CONV_U, HEAD_U = 2 * CONV_T, 2 * HEAD_T
    N_HEAD = J * CONV_U
    N_OUT = N_HEAD + H * HEAD_U
    CHUNKS = D // 512
    OUT_U = (W_A + W_B) // (2 * P)
    N_END = N_OUT + CHUNKS * OUT_U

    COL_Q, COL_F, COL_V, COL_GA = 0, W_A, 2 * W_A, 3 * W_A
    COL_U, COL_UG, COL_GB = 4 * W_A, 4 * W_A + W_B, 4 * W_A + 2 * W_B
    CONV_COLS = (COL_UG, COL_U, COL_GB)
    HEAD_COLS = (COL_F, COL_Q, COL_V, COL_GA)

    LEVELS = [64, 32, 16, 8, 4, 2]
    NL = len(LEVELS)
    COPIES = NL + 1
    HALF = T // 2
    PAIRS = [0, 1, 2] + [H // 2 + q for q in range(J // 2)] + [3]
    MIX_AT = [2 * q + r for q in PAIRS for r in range(2)]

    ctx = ExitStack()
    with ctx:
        def sb(name, shape, dt=fp32):
            return ctx.enter_context(nc.sbuf_tensor(name, shape, dt))

        def sems(names):
            return [ctx.enter_context(nc.semaphore(n)) for n in names.split()]

        h_hi = sb("h_hi", [P, KT * T], fp32r)
        h_lo = sb("h_lo", [P, KT * T], fp32r)
        w_raw = sb("w_raw", [P, RING * UW])
        w_hi = sb("w_hi", [P, RING * UW], fp32r)
        w_lo = sb("w_lo", [P, RING * UW], fp32r)
        mix = sb("mix", [P, KT * T])
        gates = sb("gates", [P, J * T])
        work = sb("work", [P, 21 * T])

        def part(n, k=1):
            return work[:, n * T:(n + k) * T]

        t1, t2, t3, t4 = (part(n) for n in range(4))
        bcum, key, qry, kmod = (part(n) for n in range(4, 8))
        lev = [part(8 + n) for n in range(NL)]
        kdec, qdec, vals, probs, sgate, lnr = (part(n) for n in range(14, 20))
        state = part(20)
        PADW = TAPS - 1 + T
        apad = [work[:, 10 * T + r * PADW:10 * T + (r + 1) * PADW] for r in range(2)]
        glu = kdec
        grow = work[0:1, 0:D]
        stage = work[:, 4 * T:4 * T + 3 * P]
        ident = sb("ident", [P, P])
        ones = sb("ones", [P, P])
        mask = sb("mask", [P, NL * HALF + T], i8)
        NPAR = TAPS + 4
        par = sb("par", [P, NPAR * J + 1])
        par3 = par[:, 0:NPAR * J].rearrange("p (n j) -> p n j", j=J)
        HGC = NPAR * J
        tap = sb("tap", [P, 2 * (TAPS + 1)])
        lnp = sb("lnp", [P, 2])
        lbw = sb("lbw", [P, 4 * H])
        lbp = sb("lbp", [P, 3 * H])
        hcur = sb("hcur", [P, 3])
        ebl = sb("ebl", [P, TT])
        ssq = sb("ssq", [P, TT * CHUNKS])
        rst = sb("rst", [P, 2 * TT])
        epsb = sb("epsb", [P, 1])
        EPSB = epsb[:, 0:1]

        banks = ctx.enter_context(nc.psum_tensor("banks", [P, 8 * 512], fp32))

        def bank(n, k=1):
            return banks[:, n * 512:(n + k) * 512]

        def x_banks(tt):
            return bank(0, 4) if tt == 1 else bank(4, 4)

        LV0, LV1, XB, OB = bank(4), bank(5), bank(6), bank(7)

        (x_in0, x_in1, x_in2, x_in3, gain_t, gain_in, par_in, res_in, stored) = sems(
            "x_in0 x_in1 x_in2 x_in3 gain_t gain_in par_in res_in stored")
        x_in = [x_in0, x_in1, x_in2, x_in3]
        raw_in = sems("raw_in0 raw_in1 raw_in2 raw_in3")
        (hi_done, lo_done, unit_done) = sems("hi_done lo_done unit_done")
        (pool_c, ident_ready, masks_ready, par_t, par_ready, lb_v, lb_s) = sems(
            "pool_c ident_ready masks_ready par_t par_ready lb_v lb_s")
        (gain_b, eps_ready, x_ss, x_rst, x_norm, x_tr, x_hi, x_lo) = sems(
            "gain_b eps_ready x_ss x_rst x_norm x_tr x_hi x_lo")
        (ug_s, ug_taken, glu_ready, u_taken, gb_taken, tap_ready, tap_done, ysum_done) = sems(
            "ug_s ug_taken glu_ready u_taken gb_taken tap_ready tap_done ysum_done")
        (mean_done, cen_done, csq_done, vacc_done, var_done, lnr_s) = sems(
            "mean_done cen_done csq_done vacc_done var_done lnr_s")
        (ln_x, ln_v, ln_s, ln_sig) = sems("ln_x ln_v ln_s ln_sig")
        (gate_taken, gate_s, gate_ls, gate_sig, gate_ready) = sems(
            "gate_taken gate_s gate_ls gate_sig gate_ready")
        (hc_ready, f_s, f_v, f_la, key_ready, q_taken, v_taken) = sems(
            "hc_ready f_s f_v f_la key_ready q_taken v_taken")
        (pair_d, pair_e, lev_d, lev_e, lev_ready, kdec_e, kdec_ready, qdec_e, qdec_ready, ebl_ready) = sems(
            "pair_d pair_e lev_d lev_e lev_ready kdec_e kdec_ready qdec_e qdec_ready ebl_ready")
        (lev_done, vt_done, vt_taken, kt_done, kt_taken, probs_done) = sems(
            "lev_done vt_done vt_taken kt_done kt_taken probs_done")
        (st_done, st_v, o_done, osq_done, norm_done, rs_s, on_done, head_done) = sems(
            "st_done st_v o_done osq_done norm_done rs_s on_done head_done")
        (mhi_done, mlo_done, y_mm, y_taken, y_sq, y_ssum, y_rs, y_out) = sems(
            "mhi_done mlo_done y_mm y_taken y_sq y_ssum y_rs y_out")

        block = ctx.enter_context(nc.Block())

        def cut(t, m, odd):
            return t.rearrange("p (g two m) -> p g two m", two=2, m=m)[:, :, odd, :]

        def pair_exp(first):
            return (t4 if first else t2)[:, 0:HALF]

        def runs(t, m):
            return t.rearrange("p (g m) -> p g m", m=m)

        def held(eng, value):
            return value if isinstance(value, int) else eng.to_reg(value)

        @block.sync
        def _(sp):
            def load_unit(n, slot, src, width):
                sp.dma_start(w_raw[:, slot * UW:(slot + 1) * UW].rearrange("p (k c) -> p k c", c=width),
                             src.rearrange("(k p) c -> p k c", p=P)).then_inc(raw_in[slot], 16)

            def in_unit(n, slot, half, col):
                load_unit(n, slot, w_in[0, half * UW:(half + 1) * UW, ds(col, P)], P)

            def conv_loads(i, first=False):
                for r in range(2):
                    for s in range(CONV_U):
                        m = CONV_U * r + s
                        n = 2 * CONV_U * i + m
                        if first and m in (2, 3):
                            x_load(m)
                        if not (first and m < RING):
                            cut_before = held(sp, n - RING + 1)
                            sp.wait_ge(raw_in[m % RING], 16)
                            sp.wait_ge(lo_done, cut_before)
                        in_unit(n, m % RING, s % 2, CONV_COLS[s // 2] + (2 * i + r) * P)

            def x_load(tt):
                sp.dma_start(mix[:, tt * D:(tt + 1) * D], x[0, tt * P:(tt + 1) * P, :]).then_inc(x_in[tt], 16)

            x_load(0)
            x_load(1)
            conv_loads(0, first=True)
            with sp.Fori(1, J // 2) as i:
                conv_loads(i)
            with sp.Fori(0, H) as h:
                for u in range(HEAD_U):
                    n = N_HEAD + HEAD_U * h + u
                    cut_before = held(sp, n - RING + 1)
                    sp.wait_ge(raw_in[u % RING], 16)
                    sp.wait_ge(lo_done, cut_before)
                    in_unit(n, u % RING, u % 2, HEAD_COLS[u // 2] + h * P)
            with sp.Fori(0, CHUNKS) as c:
                for s in range(OUT_U):
                    n = N_OUT + OUT_U * c + s
                    cut_before = held(sp, n - RING + 1)
                    sp.wait_ge(raw_in[s % RING], 16)
                    sp.wait_ge(lo_done, cut_before)
                    load_unit(n, s % RING, w_out[0, 2 * P * PAIRS[s]:2 * P * (PAIRS[s] + 1), ds(c * 512, 512)], 512)
            for tt in range(TT):
                sp.wait_ge(y_out, tt + 1)
                sp.dma_start(out[0, tt * P:(tt + 1) * P, :], mix[:, tt * D:(tt + 1) * D]).then_inc(stored, 16)
            sp.wait_ge(stored, 16 * TT)

        @block.gpsimd
        def _(pool):
            g = nc.gpsimd
            count = [0]

            def link(ins):
                count[0] += 1
                ins.then_inc(pool_c, 1)
                pool.wait_ge(pool_c, count[0])

            link(g.memset(ones[:], 1.0))
            link(g.memset(ident[:], 1.0))
            link(g.affine_select(out=ident[:], in_=ident[:], pattern=[[-1, P]], compare_op=ALU.is_equal,
                                 fill=0.0, base=0, channel_multiplier=1))
            g.memset(mask[:], 1).then_inc(ident_ready, 1)

            def lo_unit(n, s):
                pool.wait_ge(hi_done, n + 1)
                a = slice(s * UW, (s + 1) * UW)
                g.tensor_tensor(w_lo[:, a], w_raw[:, a], w_hi[:, a].bitcast(fp32), ALU.subtract).then_inc(lo_done, 1)

            def mask_step(n, second):
                if n < NL:
                    m = LEVELS[n]
                    w = mask[:, n * HALF:(n + 1) * HALF].rearrange("p (b g m) -> p b g m", b=TT, m=m)
                    first, then = [[0, TT], [-2 * m, P // (2 * m)], [0, m]], [[0, TT], [2 * m, P // (2 * m)], [0, m]]
                    base = m - 1
                else:
                    w = mask[:, NL * HALF:NL * HALF + T].rearrange("p (b g m) -> p b g m", b=TT, m=2)
                    first, then = [[0, TT], [-2, P // 2], [0, 2]], [[0, TT], [2, P // 2], [1, 2]]
                    base = 0
                if not second:
                    return g.affine_select(out=w, in_=w, pattern=first, compare_op=ALU.is_ge, fill=0.0, base=0,
                                           channel_multiplier=1)
                return g.affine_select(out=w, in_=w, pattern=then, compare_op=ALU.is_ge, fill=0.0, base=base,
                                       channel_multiplier=-1)

            PEEL = 3
            for n in range(PEEL * RING):
                lo_unit(n, n % RING)
                if 4 <= n < 4 + NL + 1:
                    link(mask_step(n - 4, False))
                    link(mask_step(n - 4, True))
            g.memset(probs, 0.0).then_inc(masks_ready, 1)
            with pool.Fori(PEEL, N_END // RING) as i:
                for s in range(RING):
                    lo_unit(RING * i + s, s)

        @block.scalar
        def _(act):
            A = nc.scalar.activation

            def hi_unit(n, slot, q, first=False):
                act.wait_ge(raw_in[slot], 16 * (q + 1))
                if not first:
                    act.wait_ge(unit_done, n - RING + 1)
                a = slice(slot * UW, (slot + 1) * UW)
                A(w_hi[:, a], w_raw[:, a], ACT.Copy).then_inc(hi_done, 1)

            def softplus_of_abs(src, tmp, sem, base):
                A(tmp, src, ACT.Abs).then_inc(sem, 1)
                act.wait_ge(sem, base + 1)
                A(tmp, tmp, ACT.Exp, scale=-1.0).then_inc(sem, 1)
                act.wait_ge(sem, base + 2)
                A(tmp, tmp, ACT.Ln, bias=1.0).then_inc(sem, 1)

            nc.scalar.preload_act_table_set("natural_log_exp_and_others")
            act.dma_start(grow, pre_norm_g).then_inc(gain_in, 16)
            dwr = dw_kernel[0].rearrange("w (j c) -> (w j) c", c=P)
            R1 = TAPS * J - P
            act.dma_start(stage[:, 0:P], dwr[0:P, :]).then_inc(par_in, 16)
            act.dma_start(stage[0:R1, P:2 * P], dwr[P:TAPS * J, :]).then_inc(par_in, 16)
            act.dma_start(stage[R1:R1 + J, P:2 * P], dw_bias[0].rearrange("(j c) -> j c", c=P)).then_inc(par_in, 16)
            for n, v in enumerate((conv_ln_g, conv_ln_b, lb_logits)):
                act.dma_start(stage[n * J:(n + 1) * J, 2 * P:3 * P], v[0].rearrange("(j c) -> j c", c=P)).then_inc(par_in, 16)
            act.dma_start(stage[3 * J:3 * J + 1, 2 * P:3 * P], hg_norm_g).then_inc(par_in, 16)

            def x_stats(tt):
                act.wait_ge(x_in[tt], 16)
                A(gates[:, D:2 * D], mix[:, tt * D:(tt + 1) * D], ACT.Square, accum_out=ssq[:, tt:tt + 1]).then_inc(x_ss, 1)
                act.wait_ge(x_ss, 2 * tt + 1)
                A(rst[:, tt:tt + 1], ssq[:, tt:tt + 1], ACT.Ln, scale=1.0 / D, bias=EPSB).then_inc(x_ss, 1)
                act.wait_ge(x_ss, 2 * tt + 2)
                A(rst[:, tt:tt + 1], rst[:, tt:tt + 1], ACT.Exp, scale=-0.5).then_inc(x_rst, 1)

            def x_hi_part(tt):
                act.wait_ge(x_tr, tt + 1)
                A(h_hi[:, :].rearrange("p (k t) -> p k t", t=T)[:, :, tt * P:(tt + 1) * P],
                  x_banks(tt).rearrange("p (k t) -> p k t", t=P), ACT.Copy).then_inc(x_hi, 1)

            act.wait_ge(eps_ready, 1)
            x_stats(0)
            act.wait_ge(gain_t, 1)
            A(gates[:, 0:D], bank(0, 4), ACT.Copy).then_inc(gain_b, 1)
            x_stats(1)
            x_hi_part(0)
            hi_unit(0, 0, 0, first=True)
            x_hi_part(1)
            hi_unit(1, 1, 0, first=True)
            x_stats(2)
            hi_unit(2, 2, 0, first=True)
            x_hi_part(2)
            x_stats(3)
            hi_unit(3, 3, 0, first=True)
            x_hi_part(3)
            act.wait_ge(lb_v, 1)
            A(lbw[:, 0:H], lbw[:, 0:H], ACT.Exp).then_inc(lb_s, 1)
            act.wait_ge(lb_v, 5)
            A(lbp[:, 0:H], lbw[:, H:2 * H], ACT.Ln, scale=-1.0, bias=1.0).then_inc(lb_s, 1)
            A(lbw[:, 3 * H:4 * H], lbw[:, 2 * H:3 * H], ACT.Ln).then_inc(lb_s, 1)

            def take_gb(j):
                act.wait_ge(unit_done, CONV_U * (j + 1))
                A(gates[:, ds(j * T, T)], bank(gb_bank[0]), ACT.Copy).then_inc(gb_taken, 1)

            def conv_channel(j, r, q0, first, start):
                for s in range(CONV_U):
                    m = CONV_U * r + s + AHEAD
                    if not (start and m < RING):
                        hi_unit(CONV_U * j + s + AHEAD, m % RING, q0 + m // RING)
                    if s == 0 and not first:
                        gb_bank[0] = (3 * (r + 1) + 2) % 2
                        take_gb(j - 1)
                    if s == 2:
                        act.wait_ge(unit_done, CONV_U * j + 2)
                        if not first:
                            act.wait_ge(u_taken, j)
                        softplus_of_abs(bank((3 * r) % 2), glu, ug_s, 3 * j)
                    if s == 3:
                        act.wait_ge(ug_taken, j + 1)
                        A(glu, glu, ACT.Exp).then_inc(glu_ready, 1)

            gb_bank = [0]
            conv_channel(0, 0, 0, True, True)
            conv_channel(1, 1, 0, False, False)
            with act.Fori(1, J // 2) as i:
                conv_channel(2 * i, 0, 3 * i, False, False)
                conv_channel(2 * i + 1, 1, 3 * i, False, False)

            def ln_square(j):
                act.wait_ge(cen_done, J)
                if j >= 2:
                    act.wait_ge(vacc_done, j - 1)
                A((t1, t2)[j % 2], mix[:, (H + j) * T:(H + j + 1) * T], ACT.Square).then_inc(csq_done, 1)

            def ln_rstd():
                act.wait_ge(var_done, 1)
                A(lnr, bank(3), ACT.Ln, scale=1.0 / W_B, bias=EPSB).then_inc(lnr_s, 1)
                act.wait_ge(lnr_s, 1)
                A(lnr, lnr, ACT.Exp, scale=-0.5).then_inc(lnr_s, 1)

            def ln_tile(j, s):
                if s == 0:
                    act.wait_ge(ln_v, 7 * j + 2)
                    A(t3, t1, ACT.Abs).then_inc(ln_s, 1)
                    A(t4, gates[:, ds(j * T, T)], ACT.Abs).then_inc(ln_s, 1)
                    act.wait_ge(ln_s, 4 * j + 2)
                    A(part(2, 2), part(2, 2), ACT.Exp, scale=-1.0).then_inc(ln_s, 1)
                    act.wait_ge(ln_s, 4 * j + 3)
                    A(part(2, 2), part(2, 2), ACT.Ln, bias=1.0).then_inc(ln_s, 1)
                if s == 1:
                    act.wait_ge(ln_v, 7 * j + 5)
                    A(t3, t3, ACT.Exp).then_inc(ln_sig, 1)

            def own(h, u, first):
                base = N_HEAD + HEAD_U * h
                if u == 2:
                    act.wait_ge(unit_done, base + 2)
                    if not first:
                        act.wait_ge(head_done, h - 1) if not isinstance(h, int) or h > 1 else None
                    softplus_of_abs(bank(0), t1, f_s, 3 * h)
                if u == 3:
                    act.wait_ge(f_v, 8 * h + 2)
                    if not first:
                        act.wait_ge(kdec_ready, h)
                        act.wait_ge(qdec_ready, h)
                    A(key, t3, ACT.Exp, scale=-1.0, bias=hcur[:, 0:1]).then_inc(key_ready, 1)
                    A(t1, t2, ACT.Abs, bias=hcur[:, 2:3]).then_inc(f_la, 1)
                    act.wait_ge(f_la, 3 * h + 1)
                    A(t1, t1, ACT.Exp, scale=-1.0).then_inc(f_la, 1)
                    act.wait_ge(f_la, 3 * h + 2)
                    A(t1, t1, ACT.Ln, bias=1.0).then_inc(f_la, 1)
                if u == 4:
                    act.wait_ge(unit_done, base + 4)
                    if not first:
                        act.wait_ge(lev_done, 4 * h - 3)
                    A(qry, bank(1), ACT.Copy, scale=Q_SCALE).then_inc(q_taken, 1)
                    for n in range(4):
                        act.wait_ge(lev_d, 7 * h + n + 1)
                        A(lev[n], lev[n], ACT.Exp).then_inc(lev_e, 1)
                if u == 5:
                    for n in (4, 5):
                        act.wait_ge(lev_d, 7 * h + n + 1)
                        A(lev[n], lev[n], ACT.Exp).then_inc(lev_e, 1)
                    act.wait_ge(lev_d, 7 * h + 7)
                    A(cut(kmod, 1, 1), cut(kmod, 1, 1), ACT.Exp).then_inc(lev_e, 1)
                    A(cut(kmod, 1, 0), cut(key, 1, 0), ACT.Copy).then_inc(lev_e, 1)
                    if not first:
                        act.wait_ge(st_done, h)
                        act.wait_ge(st_v, 3 * h)
                    for c in range(TT - 1):
                        A(kdec[:, c * P:(c + 1) * P], bcum[:, c * P:(c + 1) * P], ACT.Exp, scale=-1.0,
                          bias=bcum[:, (c + 1) * P - 1:(c + 1) * P]).then_inc(kdec_e, 1)
                    A(ebl[:, 0:TT - 1], bcum.rearrange("p (c t) -> p c t", t=P)[:, 0:TT - 1, P - 1], ACT.Exp).then_inc(ebl_ready, 1)
                if u == 6:
                    if not first:
                        act.wait_ge(o_done, h)
                    A(qdec[:, P:T], bcum[:, P:T], ACT.Exp).then_inc(qdec_e, 1)
                    act.wait_ge(unit_done, base + 6)
                    A(vals, bank(0), ACT.Copy).then_inc(v_taken, 1)
                    act.wait_ge(pair_d, h + 1)
                    A(pair_exp(first), pair_exp(first), ACT.Exp).then_inc(pair_e, 1)

            def late(g, u, first):
                if u == 0:
                    act.wait_ge(unit_done, N_HEAD + HEAD_U * (g + 1))
                    if not first:
                        act.wait_ge(head_done, g)
                    A(sgate, bank(1), ACT.Copy).then_inc(gate_taken, 1)
                    act.wait_ge(gate_taken, g + 1)
                    softplus_of_abs(sgate, t4, gate_s, 3 * g)
                if u == 1:
                    act.wait_ge(vt_done, g + 1)
                    A(vals, XB, ACT.Copy).then_inc(vt_taken, 1)
                    act.wait_ge(gate_ls, g + 1)
                    A(t4, t4, ACT.Exp).then_inc(gate_sig, 1)
                if u == 2:
                    act.wait_ge(kt_done, g + 1)
                    A(kdec[:, 0:T - P], XB[:, 0:T - P], ACT.Copy).then_inc(kt_taken, 1)
                if u == 6:
                    act.wait_ge(o_done, g + 1)
                    act.wait_ge(gate_ready, g + 1)
                    act.wait_ge(ln_v, 7 * g + 6)
                    A(t4, OB, ACT.Square).then_inc(osq_done, 1)
                if u == 7:
                    act.wait_ge(norm_done, g + 1)
                    A(t1, XB, ACT.Ln, scale=1.0 / P, bias=EPSB).then_inc(rs_s, 1)
                    act.wait_ge(rs_s, 2 * g + 1)
                    A(t1, t1, ACT.Exp, scale=-0.5).then_inc(rs_s, 1)

            def head_step(h, u, q0):
                base = N_HEAD + HEAD_U * h
                hi_unit(base + u + AHEAD, (u + AHEAD) % RING, q0 + (u + AHEAD) // RING)

            for u in range(HEAD_U):
                head_step(0, u, N_HEAD // RING)
                if u == 0:
                    gb_bank[0] = 1
                    take_gb(J - 1)
                own(0, u, True)
                if u >= 6:
                    for j in range(J // 2 * (u - 6), J // 2 * (u - 5)):
                        ln_square(j)

            def head_rest(h, first):
                for u in range(HEAD_U):
                    head_step(h, u, N_HEAD // RING + 2 * h)
                    if first and u == 0:
                        ln_rstd()
                    late(h - 1, u, first)
                    own(h, u, False)
                    if u in (4, 5):
                        ln_tile(h - 1, u - 4)

            head_rest(1, True)
            with act.Fori(2, H) as h:
                head_rest(h, False)

            def mix_hi(at):
                m = MIX_AT[at]
                act.wait_ge(unit_done, N_OUT - 1 if at < HK else N_OUT)
                if m < H:
                    act.wait_ge(head_done, m + 1)
                else:
                    act.wait_ge(ln_v, 7 * (m - H + 1))
                A(h_hi[:, at * T:(at + 1) * T], mix[:, m * T:(m + 1) * T], ACT.Copy).then_inc(mhi_done, 1)

            def take_sq(c, tt):
                act.wait_ge(y_taken, TT * c + tt + 1)
                if c:
                    act.wait_ge(y_sq, TT * (c - 1) + tt + 1)
                A(part(tt), bank(4 * (c % 2) + tt), ACT.Square, accum_out=ssq[:, tt * CHUNKS + c:tt * CHUNKS + c + 1]).then_inc(y_sq, 1)

            def out_hi(c, s):
                n = N_OUT + OUT_U * c + s + AHEAD
                if n < N_END:
                    hi_unit(n, n % RING, n // RING)

            for at in range(6):
                mix_hi(at)
            for s in range(OUT_U):
                out_hi(0, s)
                late(H - 1, s, False)
                if s in (2, 3):
                    ln_tile(J - 1, s - 2)
                for at in {0: (6, 7), 1: (8, 9), 2: (10, 11), 3: (12,), 5: (13, 14), 7: (15,)}.get(s, ()):
                    mix_hi(at)
                if s == 5:
                    act.dma_start(gates[:, 0:D], post_norm_g[0].partition_broadcast(P)).then_inc(gain_in, 16)
            for c in range(1, CHUNKS):
                for s in range(OUT_U):
                    out_hi(c, s)
                    if c == 1 and s == 0:
                        act.wait_ge(mlo_done, KT)
                        for tt in range(TT):
                            act.dma_start(work[:, 4 * T + tt * D:4 * T + (tt + 1) * D], x[0, tt * P:(tt + 1) * P, :]).then_inc(res_in, 16)
                    if s in (1, 2):
                        take_sq(c - 1, 2 * s - 2)
                        take_sq(c - 1, 2 * s - 1)
            for tt in range(TT):
                take_sq(CHUNKS - 1, tt)
                act.wait_ge(y_ssum, tt + 1)
                A(rst[:, tt:tt + 1], rst[:, TT + tt:TT + tt + 1], ACT.Ln, scale=1.0 / D, bias=EPSB).then_inc(y_rs, 1)
                act.wait_ge(y_rs, 2 * tt + 1)
                A(rst[:, tt:tt + 1], rst[:, tt:tt + 1], ACT.Exp, scale=-0.5).then_inc(y_rs, 1)

        @block.vector
        def _(dve):
            V = nc.vector
            V.memset(epsb[:], EPS).then_inc(eps_ready, 1)
            V.memset(apad[0][:, 0:TAPS - 1], 0.0)
            V.memset(apad[1][:, 0:TAPS - 1], 0.0)

            def x_scale(tt):
                dve.wait_ge(x_rst, tt + 1)
                if tt == 0:
                    dve.wait_ge(gain_b, 1)
                a = mix[:, tt * D:(tt + 1) * D]
                V.scalar_tensor_tensor(a, a, rst[:, tt:tt + 1], gates[:, 0:D], ALU.mult, ALU.mult).then_inc(x_norm, 1)

            def x_lo_part(tt):
                dve.wait_ge(x_hi, tt + 1)
                v = slice(tt * P, (tt + 1) * P)
                V.tensor_tensor(h_lo[:, :].rearrange("p (k t) -> p k t", t=T)[:, :, v],
                                x_banks(tt).rearrange("p (k t) -> p k t", t=P),
                                h_hi[:, :].rearrange("p (k t) -> p k t", t=T)[:, :, v].bitcast(fp32),
                                ALU.subtract).then_inc(x_lo, 1)

            x_scale(0)
            x_scale(1)
            x_lo_part(0)
            x_lo_part(1)
            x_scale(2)
            x_lo_part(2)
            x_scale(3)
            dve.wait_ge(par_t, 1)
            V.tensor_copy(par[:, :], bank(2)[:, 0:NPAR * J + 1]).then_inc(par_ready, 1)
            dve.wait_ge(par_ready, 1)
            lgt = par3[:, TAPS + 3, :]
            V.tensor_tensor(lbw[:, 0:H], lgt, lgt, ALU.subtract).then_inc(lb_v, 1)
            x_lo_part(3)
            dve.wait_ge(lb_s, 1)
            V.reciprocal(lbw[:, H:2 * H], lbw[:, 0:H]).then_inc(lb_v, 1)
            dve.wait_ge(lb_v, 2)
            V.tensor_tensor(lbw[:, 0:H], lbw[:, 0:H], lbw[:, H:2 * H], ALU.mult).then_inc(lb_v, 1)
            dve.wait_ge(lb_v, 3)
            V.tensor_tensor(lbw[:, H:2 * H], lbw[:, 0:H], lbw[:, 0:H], ALU.subtract).then_inc(lb_v, 1)
            dve.wait_ge(lb_v, 4)
            V.tensor_scalar(lbw[:, 2 * H:3 * H], lbw[:, H:2 * H], LB_FLOOR, 2.0 ** 50, ALU.max, ALU.mult).then_inc(lb_v, 1)
            dve.wait_ge(lb_s, 3)
            V.tensor_scalar(lbp[:, H:2 * H], lbw[:, 3 * H:4 * H], LN2_50, None, ALU.subtract).then_inc(lb_v, 1)
            dve.wait_ge(lb_v, 6)
            V.tensor_tensor(lbp[:, 2 * H:3 * H], lbp[:, 0:H], lbp[:, H:2 * H], ALU.subtract).then_inc(lb_v, 1)

            def conv_taps(j, r, a, b):
                acc = bank(2 + r)
                tp = tap[:, r * (TAPS + 1):(r + 1) * (TAPS + 1)]
                for w in range(a, b):
                    src = apad[r][:, w:w + T]
                    if w == 0:
                        V.tensor_scalar(acc, src, tp[:, 0:1], tp[:, TAPS:TAPS + 1], ALU.mult, ALU.add).then_inc(tap_done, 1)
                    else:
                        dve.wait_ge(tap_done, TAPS * j + w)
                        dst = acc if w < TAPS - 1 else mix[:, ds((H + j) * T, T)]
                        V.scalar_tensor_tensor(dst, src, tp[:, w:w + 1], acc, ALU.mult, ALU.add).then_inc(tap_done, 1)

            def add_to_sum(j, first):
                dve.wait_ge(tap_done, TAPS * (j + 1))
                y = mix[:, ds((H + j) * T, T)]
                if first:
                    V.tensor_copy(lnr, y).then_inc(ysum_done, 1)
                else:
                    dve.wait_ge(ysum_done, j)
                    V.tensor_tensor(lnr, lnr, y, ALU.add).then_inc(ysum_done, 1)

            def finish_conv(j, r, s, first):
                a, b = ((11, 17), (17, 23), (23, 27), (27, TAPS))[s]
                conv_taps(j, r, a, b)
                if s == 3:
                    add_to_sum(j, first)

            def conv_channel(j, r, first, second):
                for s in range(CONV_U):
                    if s == 2:
                        dve.wait_ge(ug_s, 3 * (j + 1))
                        V.scalar_tensor_tensor(glu, bank((3 * r) % 2), 0.0, glu, ALU.min, ALU.subtract).then_inc(ug_taken, 1)
                    if s < 4 and not first:
                        finish_conv(j - 1, 1 - r, s, second)
                    if s == 4:
                        dve.wait_ge(glu_ready, j + 1)
                        dve.wait_ge(unit_done, CONV_U * j + 4)
                        V.tensor_tensor(apad[r][:, TAPS - 1:], bank((3 * r + 1) % 2), glu, ALU.mult).then_inc(u_taken, 1)
                        V.tensor_copy(tap[:, r * (TAPS + 1):(r + 1) * (TAPS + 1)], par3[:, 0:TAPS + 1, j]).then_inc(tap_ready, 1)
                        dve.wait_ge(u_taken, j + 1)
                        dve.wait_ge(tap_ready, j + 1)
                        conv_taps(j, r, 0, 5)
                    if s == 5:
                        conv_taps(j, r, 5, 11)

            conv_channel(0, 0, True, False)
            conv_channel(1, 1, False, True)
            with dve.Fori(1, J // 2) as i:
                conv_channel(2 * i, 0, False, False)
                conv_channel(2 * i + 1, 1, False, False)

            def centre():
                dve.wait_ge(mean_done, 1)
                for j in range(J):
                    y = mix[:, (H + j) * T:(H + j + 1) * T]
                    V.scalar_tensor_tensor(y, bank(2), -1.0 / W_B, y, ALU.mult, ALU.add).then_inc(cen_done, 1)

            def add_squares(j0, j1):
                for j in range(j0, j1):
                    dve.wait_ge(csq_done, j + 1)
                    sq = (t1, t2)[j % 2]
                    if j:
                        dve.wait_ge(vacc_done, j)
                        V.tensor_tensor(t3, t3, sq, ALU.add).then_inc(vacc_done, 1)
                    else:
                        V.tensor_copy(t3, sq).then_inc(vacc_done, 1)

            def ln_tile(j, s, first):
                y = mix[:, ds((H + j) * T, T)]
                gb = gates[:, ds(j * T, T)]
                if s == 0:
                    if first:
                        dve.wait_ge(lnr_s, 2)
                    V.tensor_copy(lnp[:, :], par3[:, TAPS + 1:TAPS + 3, j]).then_inc(ln_v, 1)
                    V.tensor_tensor(t1, y, lnr, ALU.mult).then_inc(ln_x, 1)
                    dve.wait_ge(ln_v, 7 * j + 1)
                    dve.wait_ge(ln_x, j + 1)
                    V.tensor_scalar(t1, t1, lnp[:, 0:1], lnp[:, 1:2], ALU.mult, ALU.add).then_inc(ln_v, 1)
                if s == 1:
                    dve.wait_ge(ln_s, 4 * (j + 1))
                    V.scalar_tensor_tensor(t3, t1, 0.0, t3, ALU.min, ALU.subtract).then_inc(ln_v, 1)
                    V.scalar_tensor_tensor(t4, gb, 0.0, t4, ALU.min, ALU.subtract).then_inc(ln_v, 1)
                    dve.wait_ge(ln_v, 7 * j + 4)
                    V.tensor_tensor(t3, t3, t4, ALU.add).then_inc(ln_v, 1)
                    V.tensor_tensor(t2, t1, gb, ALU.mult).then_inc(ln_v, 1)
                if s == 2:
                    dve.wait_ge(ln_sig, j + 1)
                    dve.wait_ge(ln_v, 7 * j + 6)
                    V.tensor_tensor(y, t2, t3, ALU.mult).then_inc(ln_v, 1)

            def own(h, u, first):
                base = N_HEAD + HEAD_U * h
                if u == 2:
                    if not first:
                        dve.wait_ge(f_la, 3 * h)
                    V.tensor_copy(hcur[:, :], lbp[:, :].rearrange("p (n j) -> p n j", j=H)[:, :, h]).then_inc(hc_ready, 1)
                    dve.wait_ge(f_s, 3 * (h + 1))
                    V.scalar_tensor_tensor(t2, bank(0), 0.0, t1, ALU.min, ALU.subtract).then_inc(f_v, 1)
                    V.scalar_tensor_tensor(t3, bank(0), 0.0, t1, ALU.max, ALU.add).then_inc(f_v, 1)
                if u == 3:
                    dve.wait_ge(f_la, 3 * h + 1)
                    dve.wait_ge(hc_ready, h + 1)
                    V.tensor_scalar(t2, t2, hcur[:, 0:1], hcur[:, 1:2], ALU.add, ALU.max).then_inc(f_v, 1)
                    dve.wait_ge(f_la, 3 * h + 3)
                    dve.wait_ge(f_v, 8 * h + 3)
                    V.tensor_tensor(t2, t2, t1, ALU.add).then_inc(f_v, 1)
                    dve.wait_ge(f_v, 8 * h + 4)
                    if not first:
                        dve.wait_ge(qdec_e, h)
                    for c in range(TT):
                        v = slice(c * P, (c + 1) * P)
                        V.tensor_tensor_scan(bcum[:, v], ones[:, :], t2[:, v], 0.0, ALU.mult, ALU.add).then_inc(f_v, 1)
                    dve.wait_ge(f_v, 8 * h + 8)
                    level_diffs(0, 4)
                if u == 4:
                    level_diffs(4, 6)
                    V.tensor_tensor(cut(kmod, 1, 1), cut(bcum, 1, 0), cut(bcum, 1, 1), ALU.subtract).then_inc(lev_d, 1)
                    dve.wait_ge(key_ready, h + 1)
                    level_times(h, 0, 4, 0, key)
                if u == 5:
                    dve.wait_ge(q_taken, h + 1)
                    level_times(h, 0, 4, 1, qry)
                if u == 6:
                    level_times(h, 4, 6, 0, key)
                    level_times(h, 4, 6, 1, qry)
                    dve.wait_ge(lev_e, 8 * h + 8)
                    V.tensor_tensor(cut(kmod, 1, 1), cut(kmod, 1, 1), cut(key, 1, 1), ALU.mult)
                    dve.wait_ge(kdec_e, 3 * (h + 1))
                    V.tensor_tensor(kdec[:, 0:T - P], kdec[:, 0:T - P], key[:, 0:T - P], ALU.mult).then_inc(kdec_ready, 1)
                    if not first:
                        dve.wait_ge(ln_v, 7 * h)
                    V.tensor_tensor(pair_exp(first), cut(bcum, 1, 1)[:, :, 0], cut(bcum, 1, 0)[:, :, 0], ALU.subtract).then_inc(pair_d, 1)
                if u == 7:
                    dve.wait_ge(qdec_e, h + 1)
                    V.tensor_tensor(qdec[:, P:T], qdec[:, P:T], qry[:, P:T], ALU.mult).then_inc(qdec_ready, 1)
                    dve.wait_ge(pair_e, h + 1)
                    dve.wait_ge(qdec_ready, h + 1)
                    odd = cut(qry, 1, 1)[:, :, 0]
                    V.tensor_tensor(odd, odd, pair_exp(first), ALU.mult).then_inc(lev_ready, 1)

            def level_diffs(a, b):
                for n in range(a, b):
                    m = LEVELS[n]
                    even, odd = cut(bcum, m, 0), cut(bcum, m, 1)
                    ref = even[:, :, m - 1:m].broadcast_to([P, T // (2 * m), m])
                    V.tensor_tensor(cut(lev[n], m, 0), ref, even, ALU.subtract)
                    V.tensor_tensor(cut(lev[n], m, 1), odd, ref, ALU.subtract).then_inc(lev_d, 1)

            def level_times(h, a, b, odd, what):
                for n in range(a, b):
                    m = LEVELS[n]
                    dve.wait_ge(lev_e, 8 * h + n + 1)
                    V.tensor_tensor(cut(lev[n], m, odd), cut(lev[n], m, odd), cut(what, m, odd), ALU.mult)

            def take_scores(g, k, src):
                if k:
                    copied = held(dve, COPIES * g + k)
                    dve.wait_ge(masks_ready, 1)
                    dve.wait_ge(probs_done, copied)
                if k == 0:
                    V.copy_predicated(probs, mask[:, NL * HALF:NL * HALF + T], src).then_inc(probs_done, 1)
                    return
                m = LEVELS[k - 1]
                rows = m if 2 * m == P else P
                V.copy_predicated(cut(probs[0:rows, :], m, 1), runs(mask[0:rows, (k - 1) * HALF:k * HALF], m),
                                  runs(src[0:rows, 0:HALF], m)).then_inc(probs_done, 1)

            def late(g, u, first):
                if u == 1:
                    dve.wait_ge(gate_s, 3 * (g + 1))
                    V.scalar_tensor_tensor(t4, sgate, 0.0, t4, ALU.min, ALU.subtract).then_inc(gate_ls, 1)
                if u == 2:
                    dve.wait_ge(gate_sig, g + 1)
                    V.tensor_tensor(sgate, sgate, t4, ALU.mult).then_inc(gate_ready, 1)
                if 1 <= u <= 4:
                    scored = held(dve, 4 * g + u)
                    used = held(dve, g)
                    dve.wait_ge(masks_ready, 1)
                    dve.wait_ge(lev_done, scored)
                    if u == 1 and not first:
                        dve.wait_ge(o_done, used)
                    for k, src in ((0, LV0),) if u == 1 else ((2 * u - 3, LV0), (2 * u - 2, LV1)):
                        take_scores(g, k, src)
                if u == 4:
                    dve.wait_ge(st_done, g + 1)
                    if not first:
                        dve.wait_ge(o_done, g)
                    V.tensor_copy(state[:, 0:P], XB[:, 0:P]).then_inc(st_v, 1)
                    dve.wait_ge(ebl_ready, g + 1)
                    for c in range(1, TT - 1):
                        dve.wait_ge(st_v, (TT - 1) * g + c)
                        V.scalar_tensor_tensor(state[:, c * P:(c + 1) * P], state[:, (c - 1) * P:c * P], ebl[:, c:c + 1],
                                               XB[:, c * P:(c + 1) * P], ALU.mult, ALU.add).then_inc(st_v, 1)
                if u == 7:
                    dve.wait_ge(rs_s, 2 * (g + 1))
                    V.tensor_tensor(t1, OB, t1, ALU.mult).then_inc(on_done, 1)
                    dve.wait_ge(on_done, g + 1)
                    dve.wait_ge(gate_ready, g + 1)
                    V.scalar_tensor_tensor(mix[:, ds(g * T, T)], t1, par[:, HGC:HGC + 1], sgate, ALU.mult, ALU.mult).then_inc(head_done, 1)

            for u in range(HEAD_U):
                if u < 4:
                    finish_conv(J - 1, 1, u, False)
                own(0, u, True)
                if u == 5:
                    centre()
                if u >= 6:
                    add_squares(J // 2 * (u - 6), J // 2 * (u - 5))

            dve.wait_ge(masks_ready, 1)

            def head_rest(h, first):
                for u in range(HEAD_U):
                    late(h - 1, u, first)
                    if u in (4, 5, 6):
                        ln_tile(h - 1, u - 4, first)
                    own(h, u, False)

            head_rest(1, True)
            with dve.Fori(2, H) as h:
                head_rest(h, False)

            def mix_lo(at):
                m = MIX_AT[at]
                dve.wait_ge(mhi_done, at + 1)
                a = slice(at * T, (at + 1) * T)
                V.tensor_tensor(h_lo[:, a], mix[:, m * T:(m + 1) * T], h_hi[:, a].bitcast(fp32), ALU.subtract).then_inc(mlo_done, 1)

            def take_y(c, tt):
                if tt < TT - 1 or c == CHUNKS - 1:
                    dve.wait_ge(y_mm, (TT - 1) * c + tt + 1)
                else:
                    dve.wait_ge(unit_done, N_OUT + OUT_U * (c + 1))
                V.tensor_tensor(mix[:, tt * D + c * 512:tt * D + (c + 1) * 512], bank(4 * (c % 2) + tt),
                                gates[:, c * 512:(c + 1) * 512], ALU.mult).then_inc(y_taken, 1)

            for at in range(6):
                mix_lo(at)
            for s in range(OUT_U):
                late(H - 1, s, False)
                if s in (2, 3, 4):
                    ln_tile(J - 1, s - 2, False)
                for at in {0: (6, 7), 1: (8, 9), 2: (10, 11), 3: (12,), 5: (13, 14), 7: (15,)}.get(s, ()):
                    mix_lo(at)
            dve.wait_ge(gain_in, 32)
            for c in range(CHUNKS - 1):
                for tt in range(TT):
                    take_y(c, tt)
            dve.wait_ge(res_in, 16 * TT)
            for tt in range(TT):
                take_y(CHUNKS - 1, tt)
                dve.wait_ge(y_sq, TT * (CHUNKS - 1) + tt + 1)
                V.tensor_reduce(rst[:, TT + tt:TT + tt + 1], ssq[:, tt * CHUNKS:(tt + 1) * CHUNKS], AX.X, ALU.add).then_inc(y_ssum, 1)
                dve.wait_ge(y_rs, 2 * (tt + 1))
                dve.wait_ge(y_taken, TT * (CHUNKS - 1) + tt + 1)
                a = mix[:, tt * D:(tt + 1) * D]
                V.scalar_tensor_tensor(a, a, rst[:, tt:tt + 1], work[:, 4 * T + tt * D:4 * T + (tt + 1) * D],
                                       ALU.mult, ALU.add).then_inc(y_out, 1)

        @block.tensor
        def _(pe):
            mm = nc.tensor.matmul

            pe.wait_ge(ident_ready, 1)
            pe.wait_ge(gain_in, 16)
            for k in range(D // 512):
                ins = mm(bank(k), ones[0:1, :], grow[:, k * 512:(k + 1) * 512], start=True, stop=True)
            ins.then_inc(gain_t, 1)

            def x_transposes(tt, lo_parts):
                pe.wait_ge(x_norm, tt + 1)
                if lo_parts:
                    pe.wait_ge(x_lo, lo_parts)
                for k in range(KT):
                    ins = nc.tensor.transpose(x_banks(tt)[:, k * P:(k + 1) * P],
                                              mix[:, tt * D + k * P:tt * D + (k + 1) * P], ident[:, :])
                ins.then_inc(x_tr, 1)

            def project_half(n, slot, half, b, th):
                pe.wait_ge(lo_done, n + 1)
                v = slice(th * T // 2, (th + 1) * T // 2)
                for k in range(HK):
                    kt = half * HK + k
                    wh = w_hi[:, slot * UW + k * P:slot * UW + (k + 1) * P]
                    wl = w_lo[:, slot * UW + k * P:slot * UW + (k + 1) * P]
                    hh, hl = h_hi[:, kt * T:(kt + 1) * T][:, v], h_lo[:, kt * T:(kt + 1) * T][:, v]
                    mm(bank(b)[:, v], wh, hh, start=kt == 0, stop=False)
                    mm(bank(b)[:, v], wh, hl, start=False, stop=False)
                    ins = mm(bank(b)[:, v], wl, hh, start=False, stop=kt == KT - 1)
                if th:
                    ins.then_inc(unit_done, 1)

            x_transposes(0, 0)
            x_transposes(1, 0)
            x_transposes(2, 1)
            pe.wait_ge(x_lo, 2)
            pe.wait_ge(par_in, 16 * 7)
            last = 3 * J + 1
            nc.tensor.transpose(bank(2)[:, 0:P], stage[:, 0:P], ident[:, :])
            nc.tensor.transpose(bank(2)[:, P:2 * P], stage[:, P:2 * P], ident[:, :])
            nc.tensor.transpose(bank(2)[:, 2 * P:2 * P + last], stage[0:last, 2 * P:3 * P], ident[0:last, 0:last]).then_inc(par_t, 1)
            for n in range(RING):
                if n == 2:
                    x_transposes(3, 3)
                project_half(n, n, n % 2, n // 2, 0)
            pe.wait_ge(x_lo, TT)
            for n in range(RING):
                project_half(n, n, n % 2, n // 2, 1)

            def project(n, slot, half, b):
                pe.wait_ge(lo_done, n + 1)
                for k in range(HK):
                    kt = half * HK + k
                    wh = w_hi[:, slot * UW + k * P:slot * UW + (k + 1) * P]
                    wl = w_lo[:, slot * UW + k * P:slot * UW + (k + 1) * P]
                    hh, hl = h_hi[:, kt * T:(kt + 1) * T], h_lo[:, kt * T:(kt + 1) * T]
                    mm(bank(b), wh, hh, start=kt == 0, stop=False)
                    mm(bank(b), wh, hl, start=False, stop=False)
                    ins = mm(bank(b), wl, hh, start=False, stop=kt == KT - 1)
                ins.then_inc(unit_done, 1)

            def conv_channel(j, r, first):
                for s in range(CONV_U):
                    if s == 0 and not first:
                        pe.wait_ge(u_taken, j)
                    if s == 2 and not first:
                        pe.wait_ge(gb_taken, j)
                    if s == 4:
                        pe.wait_ge(ug_taken, j + 1)
                    if first and s < RING:
                        continue
                    project(CONV_U * j + s, (CONV_U * r + s) % RING, s % 2, (3 * r + s // 2) % 2)

            conv_channel(0, 0, True)
            conv_channel(1, 1, False)
            with pe.Fori(1, J // 2) as i:
                conv_channel(2 * i, 0, False)
                conv_channel(2 * i + 1, 1, False)

            def slot(g, u, first):
                if u == 0:
                    pe.wait_ge(lev_ready, g + 1)
                    if not first:
                        pe.wait_ge(probs_done, COPIES * g)
                    for c in range(TT):
                        v = slice(c * P, (c + 1) * P)
                        ins = mm(LV0[:, v], kmod[:, v], qry[:, v], start=True, stop=True)
                    ins.then_inc(lev_done, 1)
                    pe.wait_ge(v_taken, g + 1)
                    if not first:
                        pe.wait_ge(rs_s, 2 * g)
                    for c in range(TT):
                        ins = nc.tensor.transpose(XB[:, c * P:(c + 1) * P], vals[:, c * P:(c + 1) * P], ident[:, :])
                    ins.then_inc(vt_done, 1)
                if 1 <= u <= 3:
                    pe.wait_ge(probs_done, COPIES * g + 2 * u - 1)
                    for n in (2 * u - 2, 2 * u - 1):
                        m = LEVELS[n]
                        for c in range(TT):
                            v, odd = slice(c * P, (c + 1) * P), slice(c * P // 2, (c + 1) * P // 2)
                            rows = m if 2 * m == P else P
                            ins = mm((LV0, LV1)[n % 2][0:rows, odd].rearrange("p (g m) -> p g m", m=m),
                                     lev[n][:, v][:, 0:rows], cut(lev[n][:, v], m, 1), start=True, stop=True)
                    ins.then_inc(lev_done, 1)
                if u == 1:
                    pe.wait_ge(vt_taken, g + 1)
                    pe.wait_ge(kdec_ready, g + 1)
                    for c in range(TT - 1):
                        ins = nc.tensor.transpose(XB[:, c * P:(c + 1) * P], kdec[:, c * P:(c + 1) * P], ident[:, :])
                    ins.then_inc(kt_done, 1)
                if u == 3:
                    pe.wait_ge(kt_taken, g + 1)
                    for c in range(TT - 1):
                        v = slice(c * P, (c + 1) * P)
                        ins = mm(XB[:, v], kdec[:, v], vals[:, v], start=True, stop=True)
                    ins.then_inc(st_done, 1)
                if u == 5:
                    pe.wait_ge(probs_done, COPIES * (g + 1))
                    pe.wait_ge(st_v, (TT - 1) * (g + 1))
                    pe.wait_ge(qdec_ready, g + 1)
                    if not first:
                        pe.wait_ge(head_done, g)
                    for c in range(TT):
                        v = slice(c * P, (c + 1) * P)
                        ins = mm(OB[:, v], vals[:, v], probs[:, v], start=True, stop=c == 0)
                        if c:
                            ins = mm(OB[:, v], state[:, (c - 1) * P:c * P], qdec[:, v], start=False, stop=True)
                    ins.then_inc(o_done, 1)
                if u == 6:
                    pe.wait_ge(osq_done, g + 1)
                    mm(XB, ones[:, :], t4, start=True, stop=True).then_inc(norm_done, 1)

            def head(h, first, second):
                for u in range(HEAD_U):
                    if u == 0:
                        pe.wait_ge(u_taken, J) if first else pe.wait_ge(v_taken, h)
                    if u == 2:
                        pe.wait_ge(gb_taken, J) if first else pe.wait_ge(gate_taken, h)
                    if u == 4:
                        pe.wait_ge(f_v, 8 * h + 2)
                    if u == 6:
                        pe.wait_ge(q_taken, h + 1)
                    project(N_HEAD + HEAD_U * h + u, u % RING, u % 2, (u // 2) % 2)
                    if not first:
                        slot(h - 1, u, second)
                    if first and u == 4:
                        pe.wait_ge(ysum_done, J)
                        mm(bank(2), ones[:, :], lnr, start=True, stop=True).then_inc(mean_done, 1)
                    if first and u == HEAD_U - 1:
                        pe.wait_ge(vacc_done, J)
                        mm(bank(3), ones[:, :], t3, start=True, stop=True).then_inc(var_done, 1)

            head(0, True, False)
            head(1, False, True)
            with pe.Fori(2, H) as h:
                head(h, False, False)

            def out_products(c, s, tt):
                for k in range(2):
                    a = slice((2 * s + k) * T + tt * P, (2 * s + k) * T + (tt + 1) * P)
                    w = slice((s % RING) * UW + k * 512, (s % RING) * UW + (k + 1) * 512)
                    o = bank(4 * (c % 2) + tt)
                    mm(o, h_hi[:, a], w_hi[:, w], start=s == 0 and k == 0, stop=False)
                    mm(o, h_hi[:, a], w_lo[:, w], start=False, stop=False)
                    ins = mm(o, h_lo[:, a], w_hi[:, w], start=False, stop=s == OUT_U - 1 and k == 1)
                return ins

            for c in range(CHUNKS):
                for s in range(OUT_U):
                    n = N_OUT + OUT_U * c + s
                    if N_END - n <= RING:
                        break
                    if c == 0:
                        slot(H - 1, s, False)
                    if c == 0 and s == 0:
                        pe.wait_ge(gate_taken, H)
                    if s == 0 and c >= 2:
                        pe.wait_ge(y_sq, TT * (c - 1))
                    pe.wait_ge(lo_done, n + 1)
                    if c == 0:
                        pe.wait_ge(mlo_done, 2 * s + 2)
                    for tt in range(TT):
                        ins = out_products(c, s, tt)
                        if s == OUT_U - 1 and tt < TT - 1:
                            ins.then_inc(y_mm, 1)
                    ins.then_inc(unit_done, 1)
            for tt in range(TT):
                for s in range(OUT_U - RING, OUT_U):
                    pe.wait_ge(lo_done, N_END - OUT_U + s + 1)
                    ins = out_products(CHUNKS - 1, s, tt)
                ins.then_inc(y_mm, 1)


_INS = ["x", "pre_norm_g", "post_norm_g", "w_in", "lb_logits", "hg_norm_g", "dw_kernel", "dw_bias",
        "conv_ln_g", "conv_ln_b", "w_out"]


def kernel(**inputs):
    import numpy as np
    import concourse.bacc as bacc
    from concourse.bass_utils import run_bass_kernel_spmd

    nc = bacc.Bacc("TRN2", target_bir_lowering=False, num_devices=1)
    arrays, args = {}, []
    for name in _INS:
        a = np.ascontiguousarray(inputs[name])
        arrays[f"in_{name}"] = a
        args.append(nc.dram_tensor(f"in_{name}", a.shape, mybir.dt.from_np(a.dtype), kind="ExternalInput").ap())
    shape = inputs["x"].shape
    args.append(nc.dram_tensor("out_y", shape, mybir.dt.float32, kind="ExternalOutput").ap())
    build_layer(nc, *args)
    r = run_bass_kernel_spmd(nc, [arrays], core_ids=[0])
    return r.results[0]["out_y"]
```

```python
from contextlib import ExitStack

import concourse.bass as bass
from concourse import mybir


def build_layer(nc, x, pre_norm_g, post_norm_g, w_in, lb_logits, hg_norm_g, dw_kernel, dw_bias,
                conv_ln_g, conv_ln_b, w_out, out):
    fp32, fp32r, i8 = mybir.dt.float32, mybir.dt.float32r, mybir.dt.int8
    ALU, ACT, AX = mybir.AluOpType, mybir.ActivationFunctionType, mybir.AxisListType
    ds = bass.ds
    P = 128
    _, T, D = x.shape
    W_A = lb_logits.shape[1]
    W_B = dw_bias.shape[1]
    TAPS = dw_kernel.shape[1]
    H = W_A // P
    J = W_B // P
    KT = D // P
    HK = KT // 2
    TT = T // P
    UW = HK * P
    RING = 4
    EPS, LB_FLOOR = 1e-6, 1e-30
    Q_SCALE = float(P) ** -0.5
    LN2_50 = 34.657359027997264
    WARM = 24
    AHEAD = 2

    CONV_T, HEAD_T = 3, 4
    CONV_U, HEAD_U = 2 * CONV_T, 2 * HEAD_T
    N_HEAD = J * CONV_U
    N_OUT = N_HEAD + H * HEAD_U
    CHUNKS = D // 512
    OUT_U = (W_A + W_B) // (2 * P)
    N_END = N_OUT + CHUNKS * OUT_U

    COL_Q, COL_F, COL_V, COL_GA = 0, W_A, 2 * W_A, 3 * W_A
    COL_U, COL_UG, COL_GB = 4 * W_A, 4 * W_A + W_B, 4 * W_A + 2 * W_B
    CONV_COLS = (COL_UG, COL_U)
    HEAD_COLS = (COL_F, COL_Q, COL_GB, COL_GA)
    VW = 2 * P
    VK = UW // VW

    LEVELS = {0: 64, 1: 32, 4: 4}
    MID_K, MID_Q = 2, 3
    WHOLE = 2
    RUN, GROUP = 8, 32
    GROUPS = P // GROUP
    MID_W = [GROUP - RUN * (i + 1) for i in range(3)]
    MID_AT = [GROUPS * sum(MID_W[:i]) for i in range(4)]
    MID = MID_AT[3]
    NEAR = 3 * P // 2
    NEAR_COPIES = 4
    MID_COPIES = 6
    COPIES = NEAR_COPIES + WHOLE + MID_COPIES + 1
    FOUR_MASK, TWO_MASK, NEAR_MASK = MID, MID + P // 2, MID + P
    HALF = T // 2
    PAIRS = [0, 1, 2] + [H // 2 + q for q in range(J // 2)] + [3]
    MIX_AT = [2 * q + r for q in PAIRS for r in range(2)]

    ctx = ExitStack()
    with ctx:
        def sb(name, shape, dt=fp32):
            return ctx.enter_context(nc.sbuf_tensor(name, shape, dt))

        def sems(names):
            return [ctx.enter_context(nc.semaphore(n)) for n in names.split()]

        h_hi = sb("h_hi", [P, KT * T], fp32r)
        h_lo = sb("h_lo", [P, KT * T], fp32r)
        w_raw = sb("w_raw", [P, RING * UW])
        w_hi = sb("w_hi", [P, RING * UW], fp32r)
        w_lo = sb("w_lo", [P, RING * UW], fp32r)
        mix = sb("mix", [P, KT * T])
        gates = sb("gates", [P, J * T])
        work = sb("work", [P, 20 * T + HALF])

        def part(n, k=1):
            return work[:, n * T:(n + k) * T]

        t1, t2, t3, t4 = (part(n) for n in range(4))
        bcum, key, qry, kmod = (part(n) for n in range(4, 8))
        lev = [part(8), part(9), part(10), work[:, 11 * T:12 * T + HALF], work[:, 12 * T + HALF:13 * T + HALF]]
        kdec, qdec, vals, probs, sgate, lnr, state = (
            work[:, n * T + HALF:(n + 1) * T + HALF] for n in range(13, 20))
        SQ_U = 6
        sq_slot = (SQ_U + 3) % RING
        sq_hi = w_hi[:, sq_slot * UW:sq_slot * UW + T]
        sq_lo = w_hi[:, sq_slot * UW + T:sq_slot * UW + 2 * T]
        PADW = TAPS - 1 + T
        apad = [work[:, 10 * T + r * PADW:10 * T + (r + 1) * PADW] for r in range(2)]
        glu = kdec
        grow = work[0:KT, 0:P]
        gcol = work[:, T:T + KT]
        stage = work[:, 4 * T:4 * T + 3 * P]
        ident = sb("ident", [P, P])
        ones = sb("ones", [P, P])
        ones_r = sb("ones_r", [P, P], fp32r)
        near = sb("near", [P, 3 * HALF])[:, :]
        near_even, near_odd, near_two = (near[:, n * HALF:(n + 1) * HALF] for n in range(3))
        mask = sb("mask", [P, NEAR_MASK + P], i8)
        NPAR = TAPS + 4
        par = sb("par", [P, NPAR * J + 1])
        par3 = par[:, 0:NPAR * J].rearrange("p (n j) -> p n j", j=J)
        HGC = NPAR * J
        tap = sb("tap", [P, 2 * (TAPS + 1)])
        lnp = sb("lnp", [P, 2])
        lbw = sb("lbw", [P, 4 * H])
        lbp = sb("lbp", [P, 3 * H])
        hcur = sb("hcur", [P, 3])
        ebl = sb("ebl", [P, TT])
        ssq = sb("ssq", [P, TT * CHUNKS])
        rst = sb("rst", [P, 2 * TT])
        epsb = sb("epsb", [P, 1])
        EPSB = epsb[:, 0:1]
        near_mask = mask[:, NEAR_MASK:]

        banks = ctx.enter_context(nc.psum_tensor("banks", [P, 8 * 512], fp32))

        def bank(n, k=1):
            return banks[:, n * 512:(n + k) * 512]

        def x_banks(tt):
            return bank(0, 4) if tt == 1 else bank(4, 4)

        def x_half(tt, half):
            return mix[:, tt * D + half * UW:tt * D + (half + 1) * UW].rearrange("p (k t) -> p k t", t=P)

        def h_half(h, tt, half):
            return h[:, :].rearrange("p (k t) -> p k t", t=T)[:, half * HK:(half + 1) * HK, tt * P:(tt + 1) * P]

        LV0, LV1, XB, OB = bank(4), bank(5), bank(6), bank(7)

        (x_in0, x_in1, x_in2, x_in3, gain_in, par_in, res_in, stored) = sems(
            "x_in0 x_in1 x_in2 x_in3 gain_in par_in res_in stored")
        x_in = [x_in0, x_in1, x_in2, x_in3]
        raw_in = sems("raw_in0 raw_in1 raw_in2 raw_in3")
        (hi_done, lo_done, unit_done) = sems("hi_done lo_done unit_done")
        (pool_c, ident_ready, masks_ready, par_t, par_ready, lb_v, lb_s) = sems(
            "pool_c ident_ready masks_ready par_t par_ready lb_v lb_s")
        (gain_t, gain_col, eps_ready, x_ss, x_rst, x_scaled, x_tr, x_norm, x_hi, x_lo) = sems(
            "gain_t gain_col eps_ready x_ss x_rst x_scaled x_tr x_norm x_hi x_lo")
        (ug_s, ug_taken, glu_ready, u_taken, gb_taken, tap_ready, tap_done, ysum_done) = sems(
            "ug_s ug_taken glu_ready u_taken gb_taken tap_ready tap_done ysum_done")
        (mean_done, cen_done, csq_done, vacc_done, var_done, lnr_s) = sems(
            "mean_done cen_done csq_done vacc_done var_done lnr_s")
        (ln_x, ln_v, ln_s, ln_sig) = sems("ln_x ln_v ln_s ln_sig")
        (gate_taken, gate_s, gate_ls, gate_sig, gate_ready) = sems(
            "gate_taken gate_s gate_ls gate_sig gate_ready")
        (hc_ready, f_s, f_v, f_la, key_ready, q_taken, v_taken) = sems(
            "hc_ready f_s f_v f_la key_ready q_taken v_taken")
        (lev_d, lev_e, lev_ready, kdec_e, kdec_ready, qdec_e, qdec_ready, ebl_ready) = sems(
            "lev_d lev_e lev_ready kdec_e kdec_ready qdec_e qdec_ready ebl_ready")
        (lev_done, vals_ready, kt_done, kt_taken, probs_done) = sems(
            "lev_done vals_ready kt_done kt_taken probs_done")
        (st_done, st_v, o_done, osq_done, osq_hi, norm_done, rs_s, on_done, head_done) = sems(
            "st_done st_v o_done osq_done osq_hi norm_done rs_s on_done head_done")
        (mhi_done, mlo_done, y_mm, y_taken, y_sq, y_ssum, y_rs, y_out) = sems(
            "mhi_done mlo_done y_mm y_taken y_sq y_ssum y_rs y_out")

        block = ctx.enter_context(nc.Block())

        def cut(t, m, odd):
            return t.rearrange("p (g two m) -> p g two m", two=2, m=m)[:, :, odd, :]

        def mid(t, i, blocks=TT):
            t = t.rearrange("p (c x) -> p c x", c=blocks)[:, :, MID_AT[i]:MID_AT[i + 1]]
            return t.rearrange("p c (g w) -> p c g w", g=GROUPS)

        def after(t, i, blocks=TT):
            return t.rearrange("p (c g x) -> p c g x", c=blocks, g=GROUPS)[:, :, :, RUN * (i + 1):]

        def runs(t, m):
            return t.rearrange("p (g m) -> p g m", m=m)

        def every_block(m, blocks=TT):
            return m.rearrange("p (one t) -> p one t", one=1).broadcast_to([P, blocks, m.shape[1]])

        def out_parts(tt):
            w = 512 if tt == TT - 1 else D
            return [(a, a + w) for a in range(0, D, w)]

        def run_pairs(m):
            return [(2 * m * r, m * r) for r in range(P // (2 * m))]

        def held(eng, value):
            return value if isinstance(value, int) else eng.to_reg(value)

        @block.sync
        def _(sp):
            def load_unit(n, slot, src, width):
                sp.dma_start(w_raw[:, slot * UW:(slot + 1) * UW].rearrange("p (k c) -> p k c", c=width),
                             src.rearrange("(k p) c -> p k c", p=P)).then_inc(raw_in[slot], 16)

            def in_unit(n, slot, half, col):
                load_unit(n, slot, w_in[0, half * UW:(half + 1) * UW, ds(col, P)], P)

            def conv_loads(i, first=False):
                for r in range(2):
                    for s in range(CONV_U):
                        m = CONV_U * r + s
                        n = 2 * CONV_U * i + m
                        if first and m == 2:
                            x_load(2)
                            x_load(3)
                        if first and m == RING:
                            par_loads()
                        if not (first and m < RING):
                            cut_before = held(sp, n - RING + 1)
                            sp.wait_ge(raw_in[m % RING], 16)
                            sp.wait_ge(lo_done, cut_before)
                        if s < 4:
                            in_unit(n, m % RING, s % 2, CONV_COLS[s // 2] + (2 * i + r) * P)
                        else:
                            k = VK * (2 * r + s - 4)
                            load_unit(n, m % RING, w_in[0, k * P:(k + VK) * P, ds(COL_V + i * VW, VW)], VW)

            def x_load(tt):
                sp.dma_start(mix[:, tt * D:(tt + 1) * D], x[0, tt * P:(tt + 1) * P, :]).then_inc(x_in[tt], 16)

            def par_loads():
                dwr = dw_kernel[0].rearrange("w (j c) -> (w j) c", c=P)
                R1 = TAPS * J - P
                sp.dma_start(stage[:, 0:P], dwr[0:P, :]).then_inc(par_in, 16)
                sp.dma_start(stage[0:R1, P:2 * P], dwr[P:TAPS * J, :]).then_inc(par_in, 16)
                sp.dma_start(stage[R1:R1 + J, P:2 * P], dw_bias[0].rearrange("(j c) -> j c", c=P)).then_inc(par_in, 16)
                for n, v in enumerate((conv_ln_g, conv_ln_b, lb_logits)):
                    sp.dma_start(stage[n * J:(n + 1) * J, 2 * P:3 * P], v[0].rearrange("(j c) -> j c", c=P)).then_inc(par_in, 16)
                sp.dma_start(stage[3 * J:3 * J + 1, 2 * P:3 * P], hg_norm_g).then_inc(par_in, 16)

            x_load(0)
            x_load(1)
            conv_loads(0, first=True)
            with sp.Fori(1, J // 2) as i:
                conv_loads(i)
            with sp.Fori(0, H) as h:
                for u in range(HEAD_U):
                    n = N_HEAD + HEAD_U * h + u
                    cut_before = held(sp, n - RING + 1)
                    sp.wait_ge(raw_in[u % RING], 16)
                    sp.wait_ge(lo_done, cut_before)
                    in_unit(n, u % RING, u % 2, HEAD_COLS[u // 2] + h * P)
            with sp.Fori(0, CHUNKS) as c:
                for s in range(OUT_U):
                    n = N_OUT + OUT_U * c + s
                    cut_before = held(sp, n - RING + 1)
                    sp.wait_ge(raw_in[s % RING], 16)
                    sp.wait_ge(lo_done, cut_before)
                    load_unit(n, s % RING, w_out[0, 2 * P * PAIRS[s]:2 * P * (PAIRS[s] + 1), ds(c * 512, 512)], 512)
            parts = 0
            for tt in range(TT):
                for a, b in out_parts(tt):
                    parts += 1
                    sp.wait_ge(y_out, parts)
                    sp.dma_start(out[0, tt * P:(tt + 1) * P, a:b], mix[:, tt * D + a:tt * D + b]).then_inc(stored, 16)
            sp.wait_ge(stored, 16 * parts)

        @block.gpsimd
        def _(pool):
            g = nc.gpsimd
            count = [0]

            def link(ins):
                count[0] += 1
                ins.then_inc(pool_c, 1)
                pool.wait_ge(pool_c, count[0])

            link(g.memset(ones[:], 1.0))
            link(g.memset(ident[:], 1.0))
            g.affine_select(out=ident[:], in_=ident[:], pattern=[[-1, P]], compare_op=ALU.is_equal,
                            fill=0.0, base=0, channel_multiplier=1).then_inc(ident_ready, 1)
            link(g.memset(mask[:], 1))

            def lo_unit(n, s):
                pool.wait_ge(hi_done, n + 1)
                a = slice(s * UW, (s + 1) * UW)
                g.tensor_tensor(w_lo[:, a], w_raw[:, a], w_hi[:, a].bitcast(fp32), ALU.subtract).then_inc(lo_done, 1)

            def mask_step(n, second):
                if n < 3:
                    w = mask[:, MID_AT[n]:MID_AT[n + 1]].rearrange("p (g w) -> p g w", g=GROUPS)
                    first, then = [[-GROUP, GROUPS], [0, MID_W[n]]], [[GROUP, GROUPS], [0, MID_W[n]]]
                    low, base = -RUN * n, RUN * (n + 1) - 1
                elif n < 5:
                    m, at = ((4, FOUR_MASK), (2, TWO_MASK))[n - 3]
                    w = mask[:, at:at + P // 2].rearrange("p (g m) -> p g m", m=m)
                    first, then = [[-2 * m, P // (2 * m)], [0, m]], [[2 * m, P // (2 * m)], [0, m]]
                    low, base = 0, m - 1
                else:
                    w = near_mask.rearrange("p (g m) -> p g m", m=2)
                    first, then = [[-2, P // 2], [0, 2]], [[2, P // 2], [1, 2]]
                    low, base = 0, 0
                if not second:
                    return g.affine_select(out=w, in_=w, pattern=first, compare_op=ALU.is_ge, fill=0.0, base=low,
                                           channel_multiplier=1)
                return g.affine_select(out=w, in_=w, pattern=then, compare_op=ALU.is_ge, fill=0.0, base=base,
                                       channel_multiplier=-1)

            PEEL = 3
            for n in range(PEEL * RING):
                lo_unit(n, n % RING)
                if 4 <= n < 10:
                    link(mask_step(n - 4, False))
                    link(mask_step(n - 4, True))
            g.memset(probs, 0.0).then_inc(masks_ready, 1)
            with pool.Fori(PEEL, N_END // RING) as i:
                for s in range(RING):
                    lo_unit(RING * i + s, s)

        @block.scalar
        def _(act):
            A = nc.scalar.activation

            def hi_unit(n, slot, q, first=False, squares=None):
                act.wait_ge(raw_in[slot], 16 * (q + 1))
                if squares is not None:
                    act.wait_ge(norm_done, squares)
                if not first:
                    act.wait_ge(unit_done, n - RING + 1)
                a = slice(slot * UW, (slot + 1) * UW)
                A(w_hi[:, a], w_raw[:, a], ACT.Copy).then_inc(hi_done, 1)

            def softplus_of_abs(src, tmp, sem, base):
                A(tmp, src, ACT.Abs).then_inc(sem, 1)
                act.wait_ge(sem, base + 1)
                A(tmp, tmp, ACT.Exp, scale=-1.0).then_inc(sem, 1)
                act.wait_ge(sem, base + 2)
                A(tmp, tmp, ACT.Ln, bias=1.0).then_inc(sem, 1)

            nc.scalar.preload_act_table_set("natural_log_exp_and_others")
            act.dma_start(grow, pre_norm_g[0].rearrange("(k c) -> k c", c=P)).then_inc(gain_in, 16)

            def x_stats(tt):
                act.wait_ge(x_in[tt], 16)
                A(gates[:, 0:D], mix[:, tt * D:(tt + 1) * D], ACT.Square, accum_out=ssq[:, tt:tt + 1]).then_inc(x_ss, 1)
                act.wait_ge(x_ss, 2 * tt + 1)
                A(rst[:, tt:tt + 1], ssq[:, tt:tt + 1], ACT.Ln, scale=1.0 / D, bias=EPSB).then_inc(x_ss, 1)
                act.wait_ge(x_ss, 2 * tt + 2)
                A(rst[:, tt:tt + 1], rst[:, tt:tt + 1], ACT.Exp, scale=-0.5).then_inc(x_rst, 1)

            def x_hi_part(tt, half):
                act.wait_ge(x_norm, 2 * tt + half + 1)
                A(h_half(h_hi, tt, half), x_half(tt, half), ACT.Copy).then_inc(x_hi, 1)

            act.wait_ge(eps_ready, 1)
            x_stats(0)
            x_stats(1)
            hi_unit(0, 0, 0, first=True)
            x_hi_part(0, 0)
            hi_unit(1, 1, 0, first=True)
            x_hi_part(0, 1)
            x_hi_part(1, 0)
            x_hi_part(1, 1)
            x_stats(2)
            hi_unit(2, 2, 0, first=True)
            x_stats(3)
            hi_unit(3, 3, 0, first=True)
            for tt in (2, 3):
                x_hi_part(tt, 0)
                x_hi_part(tt, 1)
            act.wait_ge(lb_v, 1)
            A(lbw[:, 0:H], lbw[:, 0:H], ACT.Exp).then_inc(lb_s, 1)
            act.wait_ge(lb_v, 5)
            A(lbp[:, 0:H], lbw[:, H:2 * H], ACT.Ln, scale=-1.0, bias=1.0).then_inc(lb_s, 1)
            A(lbw[:, 3 * H:4 * H], lbw[:, 2 * H:3 * H], ACT.Ln).then_inc(lb_s, 1)

            def take_v(i):
                act.wait_ge(unit_done, 2 * CONV_U * (i + 1))
                A(mix[:, ds(2 * i * T, 2 * T)].rearrange("p (a c k) -> p c a k", a=2, k=P),
                  bank(4, TT).rearrange("p (c n) -> p c n", n=512)[:, :, 0:VW].rearrange("p c (a k) -> p c a k", k=P), ACT.Copy).then_inc(v_taken, 1)

            def conv_channel(i, r, first):
                j = 2 * i + r
                for s in range(CONV_U):
                    m = CONV_U * r + s + AHEAD
                    if not (first and m < RING):
                        hi_unit(CONV_U * j + s + AHEAD, m % RING, 2 * CONV_U // RING * i + m // RING)
                    if s == 0 and r == 0 and not first:
                        take_v(i - 1)
                    if s == 2:
                        act.wait_ge(unit_done, CONV_U * j + 2)
                        if not first:
                            act.wait_ge(u_taken, j)
                        softplus_of_abs(bank(0), glu, ug_s, 3 * j)
                    if s == 3:
                        act.wait_ge(ug_taken, j + 1)
                        A(glu, glu, ACT.Exp).then_inc(glu_ready, 1)

            conv_channel(0, 0, True)
            conv_channel(0, 1, False)
            with act.Fori(1, J // 2) as i:
                conv_channel(i, 0, False)
                conv_channel(i, 1, False)

            def ln_square(j):
                act.wait_ge(cen_done, J)
                if j >= 2:
                    act.wait_ge(vacc_done, j - 1)
                A((t1, t2)[j % 2], mix[:, (H + j) * T:(H + j + 1) * T], ACT.Square).then_inc(csq_done, 1)

            def ln_rstd():
                act.wait_ge(var_done, 1)
                A(lnr, bank(3), ACT.Ln, scale=1.0 / W_B, bias=EPSB).then_inc(lnr_s, 1)
                act.wait_ge(lnr_s, 1)
                A(lnr, lnr, ACT.Exp, scale=-0.5).then_inc(lnr_s, 1)

            def ln_tile(j, s):
                if s == 0:
                    act.wait_ge(gb_taken, j + 1)
                    act.wait_ge(ln_v, 7 * j + 2)
                    A(t3, t1, ACT.Abs).then_inc(ln_s, 1)
                    A(t4, gates[:, ds(j * T, T)], ACT.Abs).then_inc(ln_s, 1)
                    act.wait_ge(ln_s, 4 * j + 2)
                    A(part(2, 2), part(2, 2), ACT.Exp, scale=-1.0).then_inc(ln_s, 1)
                    act.wait_ge(ln_s, 4 * j + 3)
                    A(part(2, 2), part(2, 2), ACT.Ln, bias=1.0).then_inc(ln_s, 1)
                if s == 1:
                    act.wait_ge(ln_v, 7 * j + 5)
                    A(t3, t3, ACT.Exp).then_inc(ln_sig, 1)

            def own(h, u, first):
                base = N_HEAD + HEAD_U * h
                if u == 2:
                    act.wait_ge(unit_done, base + 2)
                    if not first:
                        act.wait_ge(head_done, h - 1) if not isinstance(h, int) or h > 1 else None
                    softplus_of_abs(bank(0), t1, f_s, 3 * h)
                if u == 3:
                    act.wait_ge(f_v, 8 * h + 2)
                    if not first:
                        act.wait_ge(kdec_ready, h)
                        act.wait_ge(qdec_ready, h)
                    A(key, t3, ACT.Exp, scale=-1.0, bias=hcur[:, 0:1]).then_inc(key_ready, 1)
                    A(t1, t2, ACT.Abs, bias=hcur[:, 2:3]).then_inc(f_la, 1)
                    act.wait_ge(f_la, 3 * h + 1)
                    A(t1, t1, ACT.Exp, scale=-1.0).then_inc(f_la, 1)
                    act.wait_ge(f_la, 3 * h + 2)
                    A(t1, t1, ACT.Ln, bias=1.0).then_inc(f_la, 1)
                if u == 4:
                    act.wait_ge(unit_done, base + 4)
                    if not first:
                        act.wait_ge(lev_done, 4 * h - 3)
                    A(near_odd, cut(bank(1), 1, 1)[:, :, 0], ACT.Copy, scale=Q_SCALE)
                    A(qry, bank(1), ACT.Copy, scale=Q_SCALE).then_inc(q_taken, 1)
                    for n in range(4):
                        act.wait_ge(lev_d, 7 * h + n + 1)
                        A(lev[n], lev[n], ACT.Exp).then_inc(lev_e, 1)
                if u == 5:
                    act.wait_ge(lev_d, 7 * h + 5)
                    A(lev[4], lev[4], ACT.Exp).then_inc(lev_e, 1)
                    act.wait_ge(lev_d, 7 * h + 6)
                    even_two = near.rearrange("p (x w) -> p x w", x=3)[:, 0::2, :]
                    A(even_two, even_two, ACT.Exp).then_inc(lev_e, 1)
                    act.wait_ge(lev_d, 7 * h + 7)
                    A(cut(kmod, 1, 0), cut(kmod, 1, 0), ACT.Exp).then_inc(lev_e, 1)
                    A(cut(kmod, 1, 1), cut(key, 1, 1), ACT.Copy).then_inc(lev_e, 1)
                    if not first:
                        act.wait_ge(st_done, h)
                        act.wait_ge(st_v, 3 * h)
                    for c in range(TT - 1):
                        A(kdec[:, c * P:(c + 1) * P], bcum[:, c * P:(c + 1) * P], ACT.Exp, scale=-1.0,
                          bias=bcum[:, (c + 1) * P - 1:(c + 1) * P]).then_inc(kdec_e, 1)
                    A(ebl[:, 0:TT - 1], bcum.rearrange("p (c t) -> p c t", t=P)[:, 0:TT - 1, P - 1], ACT.Exp).then_inc(ebl_ready, 1)
                if u == 6:
                    if not first:
                        act.wait_ge(o_done, h)
                    A(qdec[:, P:T], bcum[:, P:T], ACT.Exp).then_inc(qdec_e, 1)
                    act.wait_ge(unit_done, base + 6)
                    A(gates[:, ds(h * T, T)], bank(0), ACT.Copy).then_inc(gb_taken, 1)

            def late(g, u, first, last=False):
                if u == 0:
                    act.wait_ge(unit_done, N_HEAD + HEAD_U * (g + 1))
                    if not first:
                        act.wait_ge(head_done, g)
                    A(sgate, bank(1), ACT.Copy).then_inc(gate_taken, 1)
                    act.wait_ge(gate_taken, g + 1)
                    softplus_of_abs(sgate, t4, gate_s, 3 * g)
                if u == 1:
                    act.wait_ge(v_taken, H // 2)
                    if not first:
                        act.wait_ge(o_done, g)
                    A(vals, mix[:, ds(g * T, T)], ACT.Copy).then_inc(vals_ready, 1)
                    act.wait_ge(gate_ls, g + 1)
                    A(t4, t4, ACT.Exp).then_inc(gate_sig, 1)
                if u == 2:
                    act.wait_ge(kt_done, g + 1)
                    A(kdec[:, 0:T - P], XB[:, 0:T - P], ACT.Copy).then_inc(kt_taken, 1)
                if u == SQ_U:
                    act.wait_ge(o_done, g + 1)
                    act.wait_ge(gate_ready, g + 1)
                    act.wait_ge(ln_v, 7 * g + 6)
                    A(t4, OB, ACT.Square).then_inc(osq_done, 1)
                    if not last:
                        act.wait_ge(osq_done, 2 * g + 1)
                        A(sq_hi, t4, ACT.Copy).then_inc(osq_hi, 1)
                if u == 7:
                    act.wait_ge(norm_done, g + 1)
                    A(t1, XB, ACT.Ln, scale=1.0 / P, bias=EPSB).then_inc(rs_s, 1)
                    act.wait_ge(rs_s, 2 * g + 1)
                    A(t1, t1, ACT.Exp, scale=-0.5).then_inc(rs_s, 1)

            def head_step(h, u, q0, squares=None):
                base = N_HEAD + HEAD_U * h
                hi_unit(base + u + AHEAD, (u + AHEAD) % RING, q0 + (u + AHEAD) // RING,
                        squares=squares if u == SQ_U + 1 else None)

            for u in range(HEAD_U):
                head_step(0, u, N_HEAD // RING)
                if u == 0:
                    take_v(J // 2 - 1)
                own(0, u, True)
                if u >= 6:
                    for j in range(J // 2 * (u - 6), J // 2 * (u - 5)):
                        ln_square(j)

            def head_rest(h, first):
                for u in range(HEAD_U):
                    head_step(h, u, N_HEAD // RING + 2 * h, squares=h)
                    if first and u == 0:
                        ln_rstd()
                    late(h - 1, u, first)
                    own(h, u, False)
                    if u in (4, 5):
                        ln_tile(h - 1, u - 4)

            head_rest(1, True)
            with act.Fori(2, H) as h:
                head_rest(h, False)

            def mix_hi(at):
                m = MIX_AT[at]
                act.wait_ge(unit_done, N_OUT - 1 if at < HK else N_OUT)
                if m < H:
                    act.wait_ge(head_done, m + 1)
                else:
                    act.wait_ge(ln_v, 7 * (m - H + 1))
                A(h_hi[:, at * T:(at + 1) * T], mix[:, m * T:(m + 1) * T], ACT.Copy).then_inc(mhi_done, 1)

            def take_sq(c, tt):
                if c < CHUNKS - 1:
                    act.wait_ge(y_taken, TT * c + tt + 1)
                else:
                    act.wait_ge(y_mm, (TT - 1) * c + tt + 1)
                if c:
                    act.wait_ge(y_sq, TT * (c - 1) + tt + 1)
                A(part(tt), bank(4 * (c % 2) + tt), ACT.Square, accum_out=ssq[:, tt * CHUNKS + c:tt * CHUNKS + c + 1]).then_inc(y_sq, 1)

            def out_hi(c, s):
                n = N_OUT + OUT_U * c + s + AHEAD
                if n < N_END:
                    hi_unit(n, n % RING, n // RING)

            for at in range(6):
                mix_hi(at)
            for s in range(OUT_U):
                if s:
                    out_hi(0, s)
                late(H - 1, s, False, last=True)
                if s == 0:
                    out_hi(0, s)
                if s in (2, 3):
                    ln_tile(J - 1, s - 2)
                for at in {0: (6, 7), 1: (8, 9), 2: (10, 11), 3: (12,), 5: (13, 14), 7: (15,)}.get(s, ()):
                    mix_hi(at)
                if s == 5:
                    act.dma_start(gates[:, 0:D], post_norm_g[0].partition_broadcast(P)).then_inc(gain_in, 16)
            for c in range(1, CHUNKS):
                for s in range(OUT_U):
                    out_hi(c, s)
                    if c == 1 and s == 0:
                        act.wait_ge(mlo_done, KT)
                        for tt in range(TT):
                            act.dma_start(work[:, 4 * T + tt * D:4 * T + (tt + 1) * D], x[0, tt * P:(tt + 1) * P, :]).then_inc(res_in, 16)
                    if s in (1, 2):
                        take_sq(c - 1, 2 * s - 2)
                        take_sq(c - 1, 2 * s - 1)
            for tt in range(TT):
                take_sq(CHUNKS - 1, tt)
                act.wait_ge(y_ssum, tt + 1)
                A(rst[:, tt:tt + 1], rst[:, TT + tt:TT + tt + 1], ACT.Ln, scale=1.0 / D, bias=EPSB).then_inc(y_rs, 1)
                act.wait_ge(y_rs, 2 * tt + 1)
                A(rst[:, tt:tt + 1], rst[:, tt:tt + 1], ACT.Exp, scale=-0.5).then_inc(y_rs, 1)

        @block.vector
        def _(dve):
            V = nc.vector
            V.memset(epsb[:], EPS).then_inc(eps_ready, 1)
            V.memset(apad[0][:, 0:TAPS - 1], 0.0)
            V.memset(apad[1][:, 0:TAPS - 1], 0.0)

            def x_scale(tt):
                dve.wait_ge(x_rst, tt + 1)
                for half in range(2):
                    a = mix[:, tt * D + half * UW:tt * D + (half + 1) * UW]
                    V.tensor_scalar(a, a, rst[:, tt:tt + 1], None, ALU.mult).then_inc(x_scaled, 1)

            def x_gain(tt, half):
                dve.wait_ge(x_tr, 2 * tt + half + 1)
                g = gcol[:, half * HK:(half + 1) * HK].rearrange("p (k one) -> p k one", one=1)
                V.tensor_tensor(x_half(tt, half),
                                x_banks(tt)[:, half * UW:(half + 1) * UW].rearrange("p (k t) -> p k t", t=P),
                                g.broadcast_to([P, HK, P]), ALU.mult).then_inc(x_norm, 1)

            def x_lo_part(tt, half):
                dve.wait_ge(x_hi, 2 * tt + half + 1)
                V.tensor_tensor(h_half(h_lo, tt, half), x_half(tt, half), h_half(h_hi, tt, half).bitcast(fp32),
                                ALU.subtract).then_inc(x_lo, 1)

            dve.wait_ge(ident_ready, 1)
            V.tensor_copy(ones_r[:, :], ones[:, :])
            dve.wait_ge(gain_t, 1)
            V.tensor_copy(gcol, bank(0)[:, 0:KT]).then_inc(gain_col, 1)
            dve.wait_ge(gain_col, 1)
            x_scale(0)
            x_gain(0, 0)
            x_scale(1)
            x_gain(0, 1)
            x_gain(1, 0)
            x_gain(1, 1)
            for half in range(2):
                x_lo_part(0, half)
                x_lo_part(1, half)
            x_scale(2)
            x_scale(3)
            for tt in (2, 3):
                x_gain(tt, 0)
                x_gain(tt, 1)
                x_lo_part(tt, 0)
                x_lo_part(tt, 1)
            dve.wait_ge(par_t, 1)
            V.tensor_copy(par[:, :], bank(2)[:, 0:NPAR * J + 1]).then_inc(par_ready, 1)
            dve.wait_ge(par_ready, 1)
            lgt = par3[:, TAPS + 3, :]
            V.tensor_tensor(lbw[:, 0:H], lgt, lgt, ALU.subtract).then_inc(lb_v, 1)
            dve.wait_ge(lb_s, 1)
            V.reciprocal(lbw[:, H:2 * H], lbw[:, 0:H]).then_inc(lb_v, 1)
            dve.wait_ge(lb_v, 2)
            V.tensor_tensor(lbw[:, 0:H], lbw[:, 0:H], lbw[:, H:2 * H], ALU.mult).then_inc(lb_v, 1)
            dve.wait_ge(lb_v, 3)
            V.tensor_tensor(lbw[:, H:2 * H], lbw[:, 0:H], lbw[:, 0:H], ALU.subtract).then_inc(lb_v, 1)
            dve.wait_ge(lb_v, 4)
            V.tensor_scalar(lbw[:, 2 * H:3 * H], lbw[:, H:2 * H], LB_FLOOR, 2.0 ** 50, ALU.max, ALU.mult).then_inc(lb_v, 1)
            dve.wait_ge(lb_s, 3)
            V.tensor_scalar(lbp[:, H:2 * H], lbw[:, 3 * H:4 * H], LN2_50, None, ALU.subtract).then_inc(lb_v, 1)
            dve.wait_ge(lb_v, 6)
            V.tensor_tensor(lbp[:, 2 * H:3 * H], lbp[:, 0:H], lbp[:, H:2 * H], ALU.subtract).then_inc(lb_v, 1)

            def conv_taps(j, r, a, b):
                acc = bank(2 + r)
                tp = tap[:, r * (TAPS + 1):(r + 1) * (TAPS + 1)]
                for w in range(a, b):
                    src = apad[r][:, w:w + T]
                    if w == 0:
                        V.tensor_scalar(acc, src, tp[:, 0:1], tp[:, TAPS:TAPS + 1], ALU.mult, ALU.add).then_inc(tap_done, 1)
                    else:
                        dve.wait_ge(tap_done, TAPS * j + w)
                        dst = acc if w < TAPS - 1 else mix[:, ds((H + j) * T, T)]
                        V.scalar_tensor_tensor(dst, src, tp[:, w:w + 1], acc, ALU.mult, ALU.add).then_inc(tap_done, 1)

            def add_to_sum(j, first):
                dve.wait_ge(tap_done, TAPS * (j + 1))
                y = mix[:, ds((H + j) * T, T)]
                if first:
                    V.tensor_copy(lnr, y).then_inc(ysum_done, 1)
                else:
                    dve.wait_ge(ysum_done, j)
                    V.tensor_tensor(lnr, lnr, y, ALU.add).then_inc(ysum_done, 1)

            def finish_conv(j, r, s, first):
                a, b = ((11, 17), (17, 23), (23, 27), (27, TAPS))[s]
                conv_taps(j, r, a, b)
                if s == 3:
                    add_to_sum(j, first)

            def conv_channel(j, r, first, second):
                for s in range(CONV_U):
                    if s == 2:
                        dve.wait_ge(ug_s, 3 * (j + 1))
                        V.scalar_tensor_tensor(glu, bank(0), 0.0, glu, ALU.min, ALU.subtract).then_inc(ug_taken, 1)
                    if s < 4 and not first:
                        finish_conv(j - 1, 1 - r, s, second)
                    if s == 4:
                        dve.wait_ge(glu_ready, j + 1)
                        dve.wait_ge(unit_done, CONV_U * j + 4)
                        V.tensor_tensor(apad[r][:, TAPS - 1:], bank(1), glu, ALU.mult).then_inc(u_taken, 1)
                        V.tensor_copy(tap[:, r * (TAPS + 1):(r + 1) * (TAPS + 1)], par3[:, 0:TAPS + 1, j]).then_inc(tap_ready, 1)
                        dve.wait_ge(u_taken, j + 1)
                        dve.wait_ge(tap_ready, j + 1)
                        conv_taps(j, r, 0, 5)
                    if s == 5:
                        conv_taps(j, r, 5, 11)

            conv_channel(0, 0, True, False)
            conv_channel(1, 1, False, True)
            with dve.Fori(1, J // 2) as i:
                conv_channel(2 * i, 0, False, False)
                conv_channel(2 * i + 1, 1, False, False)

            def centre():
                dve.wait_ge(mean_done, 1)
                for j in range(J):
                    y = mix[:, (H + j) * T:(H + j + 1) * T]
                    V.scalar_tensor_tensor(y, bank(2), -1.0 / W_B, y, ALU.mult, ALU.add).then_inc(cen_done, 1)

            def add_squares(j0, j1):
                for j in range(j0, j1):
                    dve.wait_ge(csq_done, j + 1)
                    sq = (t1, t2)[j % 2]
                    if j:
                        dve.wait_ge(vacc_done, j)
                        V.tensor_tensor(t3, t3, sq, ALU.add).then_inc(vacc_done, 1)
                    else:
                        V.tensor_copy(t3, sq).then_inc(vacc_done, 1)

            def ln_tile(j, s, first):
                y = mix[:, ds((H + j) * T, T)]
                gb = gates[:, ds(j * T, T)]
                if s == 0:
                    if first:
                        dve.wait_ge(lnr_s, 2)
                    V.tensor_copy(lnp[:, :], par3[:, TAPS + 1:TAPS + 3, j]).then_inc(ln_v, 1)
                    V.tensor_tensor(t1, y, lnr, ALU.mult).then_inc(ln_x, 1)
                    dve.wait_ge(ln_v, 7 * j + 1)
                    dve.wait_ge(ln_x, j + 1)
                    V.tensor_scalar(t1, t1, lnp[:, 0:1], lnp[:, 1:2], ALU.mult, ALU.add).then_inc(ln_v, 1)
                if s == 1:
                    dve.wait_ge(ln_s, 4 * (j + 1))
                    V.scalar_tensor_tensor(t3, t1, 0.0, t3, ALU.min, ALU.subtract).then_inc(ln_v, 1)
                    V.scalar_tensor_tensor(t4, gb, 0.0, t4, ALU.min, ALU.subtract).then_inc(ln_v, 1)
                    dve.wait_ge(ln_v, 7 * j + 4)
                    V.tensor_tensor(t3, t3, t4, ALU.add).then_inc(ln_v, 1)
                    V.tensor_tensor(t2, t1, gb, ALU.mult).then_inc(ln_v, 1)
                if s == 2:
                    dve.wait_ge(ln_sig, j + 1)
                    dve.wait_ge(ln_v, 7 * j + 6)
                    V.tensor_tensor(y, t2, t3, ALU.mult).then_inc(ln_v, 1)

            def own(h, u, first):
                base = N_HEAD + HEAD_U * h
                if u == 2:
                    if not first:
                        dve.wait_ge(f_la, 3 * h)
                    V.tensor_copy(hcur[:, :], lbp[:, :].rearrange("p (n j) -> p n j", j=H)[:, :, h]).then_inc(hc_ready, 1)
                    dve.wait_ge(f_s, 3 * (h + 1))
                    V.scalar_tensor_tensor(t2, bank(0), 0.0, t1, ALU.min, ALU.subtract).then_inc(f_v, 1)
                    V.scalar_tensor_tensor(t3, bank(0), 0.0, t1, ALU.max, ALU.add).then_inc(f_v, 1)
                if u == 3:
                    dve.wait_ge(f_la, 3 * h + 1)
                    dve.wait_ge(hc_ready, h + 1)
                    V.tensor_scalar(t2, t2, hcur[:, 0:1], hcur[:, 1:2], ALU.add, ALU.max).then_inc(f_v, 1)
                    dve.wait_ge(f_la, 3 * h + 3)
                    dve.wait_ge(f_v, 8 * h + 3)
                    V.tensor_tensor(t2, t2, t1, ALU.add).then_inc(f_v, 1)
                    dve.wait_ge(f_v, 8 * h + 4)
                    if not first:
                        dve.wait_ge(qdec_e, h)
                    for c in range(TT):
                        v = slice(c * P, (c + 1) * P)
                        V.tensor_tensor_scan(bcum[:, v], ones[:, :], t2[:, v], 0.0, ALU.mult, ALU.add).then_inc(f_v, 1)
                    dve.wait_ge(f_v, 8 * h + 8)
                    level_diffs(0, 4)
                if u == 4:
                    level_diffs(4, 5)
                    even, odd = cut(bcum, 1, 0), cut(bcum, 1, 1)
                    ref = cut(bcum, 2, 0)[:, :, 1:2].broadcast_to([P, T // 4, 2])
                    V.tensor_tensor(runs(near_two, 2), cut(bcum, 2, 1), ref, ALU.subtract)
                    V.tensor_tensor(near_even, even[:, :, 0], odd[:, :, 0], ALU.subtract).then_inc(lev_d, 1)
                    V.tensor_tensor(cut(kmod, 1, 0), odd, even, ALU.subtract).then_inc(lev_d, 1)
                    dve.wait_ge(key_ready, h + 1)
                    level_times(h, 0, 4, 0, key)
                if u == 5:
                    dve.wait_ge(q_taken, h + 1)
                    level_times(h, 0, 4, 1, qry)
                if u == 6:
                    level_times(h, 4, 5, 0, key)
                    level_times(h, 4, 5, 1, qry)
                    dve.wait_ge(lev_e, 8 * h + 6)
                    V.tensor_tensor(runs(near_two, 2), runs(near_two, 2), cut(qry, 2, 1), ALU.mult)
                    V.tensor_tensor(near_even, near_even, cut(qry, 1, 0)[:, :, 0], ALU.mult)
                    dve.wait_ge(lev_e, 8 * h + 8)
                    V.tensor_tensor(cut(kmod, 1, 0), cut(kmod, 1, 0), cut(key, 1, 0), ALU.mult).then_inc(lev_ready, 1)
                    dve.wait_ge(kdec_e, 3 * (h + 1))
                    V.tensor_tensor(kdec[:, 0:T - P], kdec[:, 0:T - P], key[:, 0:T - P], ALU.mult).then_inc(kdec_ready, 1)
                if u == 7:
                    dve.wait_ge(qdec_e, h + 1)
                    V.tensor_tensor(qdec[:, P:T], qdec[:, P:T], qry[:, P:T], ALU.mult).then_inc(qdec_ready, 1)

            def level_diffs(a, b):
                for n in range(a, b):
                    if n == MID_K:
                        ref = runs(bcum, RUN)[:, :, RUN - 1:RUN].broadcast_to([P, T // RUN, RUN])
                        V.tensor_tensor(runs(lev[n], RUN), ref, runs(bcum, RUN), ALU.subtract).then_inc(lev_d, 1)
                    elif n == MID_Q:
                        for i in range(3):
                            ref = after(bcum, i - 1)[:, :, :, RUN - 1:RUN].broadcast_to([P, TT, GROUPS, MID_W[i]])
                            ins = V.tensor_tensor(mid(lev[n], i), after(bcum, i), ref, ALU.subtract)
                        ins.then_inc(lev_d, 1)
                    else:
                        m = LEVELS[n]
                        even, odd = cut(bcum, m, 0), cut(bcum, m, 1)
                        ref = even[:, :, m - 1:m].broadcast_to([P, T // (2 * m), m])
                        V.tensor_tensor(cut(lev[n], m, 0), ref, even, ALU.subtract)
                        V.tensor_tensor(cut(lev[n], m, 1), odd, ref, ALU.subtract).then_inc(lev_d, 1)

            def level_times(h, a, b, odd, what):
                for n in range(a, b):
                    dve.wait_ge(lev_e, 8 * h + n + 1)
                    if n in LEVELS:
                        m = LEVELS[n]
                        V.tensor_tensor(cut(lev[n], m, odd), cut(lev[n], m, odd), cut(what, m, odd), ALU.mult)
                    elif n == MID_K and not odd:
                        V.tensor_tensor(lev[n], lev[n], what, ALU.mult)
                    elif n == MID_Q and odd:
                        for i in range(3):
                            V.tensor_tensor(mid(lev[n], i), mid(lev[n], i), after(what, i), ALU.mult)

            def take_scores(g, k, src):
                if k:
                    copied = held(dve, COPIES * g + k)
                    dve.wait_ge(masks_ready, 1)
                    dve.wait_ge(probs_done, copied)
                if k < NEAR_COPIES:
                    b, two = k // 2, k % 2
                    dst = probs[:, b * HALF:(b + 1) * HALF]
                    near_s = src[:, 0:2 * NEAR].rearrange("p (c x) -> p c x", x=NEAR)
                    if two:
                        V.copy_predicated(dst.rearrange("p (c g two m) -> p c g two m", c=2, two=2, m=2)[:, :, :, 1, :],
                                          every_block(mask[:, TWO_MASK:TWO_MASK + P // 2], 2)
                                          .rearrange("p c (g m) -> p c g m", m=2),
                                          near_s[:, :, P:].rearrange("p c (g m) -> p c g m", m=2)).then_inc(probs_done, 1)
                    else:
                        V.copy_predicated(dst.rearrange("p (c g two) -> p c two g", c=2, two=2),
                                          every_block(near_mask, 2).rearrange("p c (g two) -> p c two g", two=2),
                                          near_s[:, :, 0:P].rearrange("p c (two g) -> p c two g", two=2)).then_inc(probs_done, 1)
                    return
                k -= NEAR_COPIES
                if k < WHOLE:
                    m = LEVELS[k]
                    for s, o in run_pairs(m):
                        ins = V.tensor_copy(probs[s:s + m, :].rearrange("p (c t) -> p c t", t=P)[:, :, s + m:s + 2 * m],
                                            src[s:s + m, 0:HALF].rearrange("p (c t) -> p c t", t=P // 2)[:, :, o:o + m])
                    ins.then_inc(probs_done, 1)
                    return
                k -= WHOLE
                if k < MID_COPIES:
                    b, i = k // 3, k % 3
                    V.copy_predicated(after(probs[:, b * HALF:(b + 1) * HALF], i, 2),
                                      every_block(mask[:, MID_AT[i]:MID_AT[i + 1]], 2)
                                      .rearrange("p c (g w) -> p c g w", g=GROUPS),
                                      mid(src[:, 0:2 * MID], i, 2)).then_inc(probs_done, 1)
                    return
                m = LEVELS[4]
                V.copy_predicated(probs.rearrange("p (c g two m) -> p c g two m", c=TT, two=2, m=m)[:, :, :, 1, :],
                                  every_block(mask[:, FOUR_MASK:FOUR_MASK + P // 2]).rearrange("p c (g m) -> p c g m", m=m),
                                  src[:, 0:HALF].rearrange("p (c g m) -> p c g m", c=TT, m=m)).then_inc(probs_done, 1)

            def late(g, u, first, last=False):
                if u == 1:
                    dve.wait_ge(gate_s, 3 * (g + 1))
                    V.scalar_tensor_tensor(t4, sgate, 0.0, t4, ALU.min, ALU.subtract).then_inc(gate_ls, 1)
                if u == 2:
                    dve.wait_ge(gate_sig, g + 1)
                    V.tensor_tensor(sgate, sgate, t4, ALU.mult).then_inc(gate_ready, 1)
                if 1 <= u <= 4:
                    scored = held(dve, 4 * g + u)
                    used = held(dve, g)
                    dve.wait_ge(masks_ready, 1)
                    dve.wait_ge(lev_done, scored)
                    if u == 1 and not first:
                        dve.wait_ge(o_done, used)
                    for k0, n in {1: ((0, 2), (2, 2)), 2: ((4, 1), (5, 1)), 3: ((6, 3), (9, 3)), 4: ((12, 1),)}[u]:
                        for k in range(k0, k0 + n):
                            take_scores(g, k, LV0 if k0 in (0, 4, 6, 12) else LV1)
                if u == 4:
                    dve.wait_ge(st_done, g + 1)
                    if not first:
                        dve.wait_ge(o_done, g)
                    V.tensor_copy(state[:, 0:P], XB[:, 0:P]).then_inc(st_v, 1)
                    dve.wait_ge(ebl_ready, g + 1)
                    for c in range(1, TT - 1):
                        dve.wait_ge(st_v, (TT - 1) * g + c)
                        V.scalar_tensor_tensor(state[:, c * P:(c + 1) * P], state[:, (c - 1) * P:c * P], ebl[:, c:c + 1],
                                               XB[:, c * P:(c + 1) * P], ALU.mult, ALU.add).then_inc(st_v, 1)
                if u == SQ_U and not last:
                    dve.wait_ge(osq_hi, g + 1)
                    V.tensor_tensor(sq_lo, t4, sq_hi.bitcast(fp32), ALU.subtract).then_inc(osq_done, 1)
                if u == 7:
                    dve.wait_ge(rs_s, 2 * (g + 1))
                    V.tensor_tensor(t1, OB, t1, ALU.mult).then_inc(on_done, 1)
                    dve.wait_ge(on_done, g + 1)
                    dve.wait_ge(gate_ready, g + 1)
                    V.scalar_tensor_tensor(mix[:, ds(g * T, T)], t1, par[:, HGC:HGC + 1], sgate, ALU.mult, ALU.mult).then_inc(head_done, 1)

            for u in range(HEAD_U):
                if u < 4:
                    finish_conv(J - 1, 1, u, False)
                own(0, u, True)
                if u == 5:
                    centre()
                if u >= 6:
                    add_squares(J // 2 * (u - 6), J // 2 * (u - 5))

            dve.wait_ge(masks_ready, 1)

            def head_rest(h, first):
                for u in range(HEAD_U):
                    late(h - 1, u, first)
                    if u in (4, 5, 6):
                        ln_tile(h - 1, u - 4, first)
                    own(h, u, False)

            head_rest(1, True)
            with dve.Fori(2, H) as h:
                head_rest(h, False)

            def mix_lo(at):
                m = MIX_AT[at]
                dve.wait_ge(mhi_done, at + 1)
                a = slice(at * T, (at + 1) * T)
                V.tensor_tensor(h_lo[:, a], mix[:, m * T:(m + 1) * T], h_hi[:, a].bitcast(fp32), ALU.subtract).then_inc(mlo_done, 1)

            def take_y(c, tt):
                if c == CHUNKS - 1:
                    dve.wait_ge(y_sq, TT * c + tt + 1)
                elif tt < TT - 1:
                    dve.wait_ge(y_mm, (TT - 1) * c + tt + 1)
                else:
                    dve.wait_ge(unit_done, N_OUT + OUT_U * (c + 1))
                V.tensor_tensor(mix[:, tt * D + c * 512:tt * D + (c + 1) * 512], bank(4 * (c % 2) + tt),
                                gates[:, c * 512:(c + 1) * 512], ALU.mult).then_inc(y_taken, 1)

            for at in range(6):
                mix_lo(at)
            for s in range(OUT_U):
                late(H - 1, s, False, last=True)
                if s in (2, 3, 4):
                    ln_tile(J - 1, s - 2, False)
                for at in {1: (6, 7, 8, 9), 2: (10, 11), 3: (12,), 5: (13, 14), 7: (15,)}.get(s, ()):
                    mix_lo(at)
            dve.wait_ge(gain_in, 32)
            for c in range(CHUNKS - 1):
                for tt in range(TT):
                    take_y(c, tt)
            dve.wait_ge(res_in, 16 * TT)
            for tt in range(TT):
                dve.wait_ge(y_sq, TT * (CHUNKS - 1) + tt + 1)
                V.tensor_reduce(rst[:, TT + tt:TT + tt + 1], ssq[:, tt * CHUNKS:(tt + 1) * CHUNKS], AX.X, ALU.add).then_inc(y_ssum, 1)
                take_y(CHUNKS - 1, tt)
                dve.wait_ge(y_rs, 2 * (tt + 1))
                dve.wait_ge(y_taken, TT * (CHUNKS - 1) + tt + 1)
                for a, b in out_parts(tt):
                    y = mix[:, tt * D + a:tt * D + b]
                    V.scalar_tensor_tensor(y, y, rst[:, tt:tt + 1], work[:, 4 * T + tt * D + a:4 * T + tt * D + b],
                                           ALU.mult, ALU.add).then_inc(y_out, 1)

        @block.tensor
        def _(pe):
            mm = nc.tensor.matmul

            pe.wait_ge(ident_ready, 1)
            for _ in range(WARM):
                nc.tensor.transpose(OB[:, 0:P], ident[:, :], ident[:, :])
            pe.wait_ge(gain_in, 16)
            nc.tensor.transpose(bank(0)[:, 0:KT], grow, ident[0:KT, 0:KT]).then_inc(gain_t, 1)

            def x_transposes(tt, read):
                if read:
                    pe.wait_ge(x_norm, read)
                for k in range(KT):
                    if k % HK == 0:
                        pe.wait_ge(x_scaled, 2 * tt + k // HK + 1)
                    ins = nc.tensor.transpose(x_banks(tt)[:, k * P:(k + 1) * P],
                                              mix[:, tt * D + k * P:tt * D + (k + 1) * P], ident[:, :])
                    if k % HK == HK - 1:
                        ins.then_inc(x_tr, 1)

            def project_half(n, th):
                b, half = n // 2, n % 2
                v = slice(th * T // 2, (th + 1) * T // 2)
                pe.wait_ge(x_hi, 4 * th + half + 3)
                pe.wait_ge(lo_done, n + 1)
                for lo in range(2):
                    if lo:
                        pe.wait_ge(x_lo, 2 * half + 2 if th == 0 else 2 * TT)
                    for k in range(HK):
                        kt = half * HK + k
                        wh = w_hi[:, n * UW + k * P:n * UW + (k + 1) * P]
                        wl = w_lo[:, n * UW + k * P:n * UW + (k + 1) * P]
                        hh, hl = h_hi[:, kt * T:(kt + 1) * T][:, v], h_lo[:, kt * T:(kt + 1) * T][:, v]
                        if lo:
                            ins = mm(bank(b)[:, v], wh, hl, start=False, stop=kt == KT - 1)
                        else:
                            mm(bank(b)[:, v], wh, hh, start=kt == 0, stop=False)
                            mm(bank(b)[:, v], wl, hh, start=False, stop=False)
                if th:
                    ins.then_inc(unit_done, 1)

            x_transposes(0, 0)
            pe.wait_ge(gain_col, 1)
            x_transposes(1, 0)
            pe.wait_ge(x_norm, 4)
            project_half(0, 0)
            project_half(1, 0)
            x_transposes(2, 2)
            project_half(2, 0)
            x_transposes(3, 6)
            pe.wait_ge(par_in, 16 * 7)
            last = 3 * J + 1
            nc.tensor.transpose(bank(2)[:, 0:P], stage[:, 0:P], ident[:, :])
            nc.tensor.transpose(bank(2)[:, P:2 * P], stage[:, P:2 * P], ident[:, :])
            nc.tensor.transpose(bank(2)[:, 2 * P:2 * P + last], stage[0:last, 2 * P:3 * P], ident[0:last, 0:last]).then_inc(par_t, 1)
            project_half(3, 0)
            for n in range(RING):
                project_half(n, 1)

            def project(n, slot, half, b):
                pe.wait_ge(lo_done, n + 1)
                for k in range(HK):
                    kt = half * HK + k
                    wh = w_hi[:, slot * UW + k * P:slot * UW + (k + 1) * P]
                    wl = w_lo[:, slot * UW + k * P:slot * UW + (k + 1) * P]
                    hh, hl = h_hi[:, kt * T:(kt + 1) * T], h_lo[:, kt * T:(kt + 1) * T]
                    mm(bank(b), wh, hh, start=kt == 0, stop=False)
                    mm(bank(b), wh, hl, start=False, stop=False)
                    ins = mm(bank(b), wl, hh, start=False, stop=kt == KT - 1)
                ins.then_inc(unit_done, 1)

            def project_values(n, slot, vu):
                pe.wait_ge(lo_done, n + 1)
                for tt in range(TT):
                    o = bank(4 + tt)[:, 0:VW]
                    for k in range(VK):
                        a = slice((VK * vu + k) * T + tt * P, (VK * vu + k) * T + (tt + 1) * P)
                        w = slice(slot * UW + k * VW, slot * UW + (k + 1) * VW)
                        mm(o, h_hi[:, a], w_hi[:, w], start=vu == 0 and k == 0, stop=False)
                        mm(o, h_hi[:, a], w_lo[:, w], start=False, stop=False)
                        ins = mm(o, h_lo[:, a], w_hi[:, w], start=False, stop=vu == 3 and k == VK - 1)
                ins.then_inc(unit_done, 1)

            def conv_channel(i, r, first):
                j = 2 * i + r
                for s in range(CONV_U):
                    if first and s < RING:
                        continue
                    n = CONV_U * j + s
                    if s == 0:
                        pe.wait_ge(ug_taken, j)
                    if s == 2:
                        pe.wait_ge(u_taken, j)
                    if s >= 4:
                        if s == 4 and r == 0 and not first:
                            pe.wait_ge(v_taken, i)
                        project_values(n, (CONV_U * r + s) % RING, 2 * r + s - 4)
                    else:
                        project(n, (CONV_U * r + s) % RING, s % 2, s // 2)

            conv_channel(0, 0, True)
            conv_channel(0, 1, False)
            with pe.Fori(1, J // 2) as i:
                conv_channel(i, 0, False)
                conv_channel(i, 1, False)

            def slot(g, u, first, last=False):
                if u == 0:
                    pe.wait_ge(lev_ready, g + 1)
                    if not first:
                        pe.wait_ge(probs_done, COPIES * g)
                    for c in range(TT):
                        lv = (LV0, LV1)[c // 2][:, (c % 2) * NEAR:(c % 2 + 1) * NEAR]
                        ins = mm(lv.rearrange("p (x w) -> p x w", x=3), kmod[:, c * P:(c + 1) * P],
                                 near.rearrange("p (x c w) -> p x c w", x=3, c=TT)[:, :, c, :], start=True, stop=True)
                    ins.then_inc(lev_done, 1)
                if 1 <= u <= 3:
                    pe.wait_ge(probs_done, COPIES * g + (4, 6, 12)[u - 1])
                    for n in ((0, 1), (MID_K,), (4,))[u - 1]:
                        for c in range(TT):
                            v = slice(c * P, (c + 1) * P)
                            lv = (LV0, LV1)[n % 2][:, c * P // 2:(c + 1) * P // 2]
                            if n == MID_K:
                                ins = mm((LV0, LV1)[c // 2][:, (c % 2) * MID:(c % 2 + 1) * MID], lev[MID_K][:, v],
                                         lev[MID_Q][:, c * MID:(c + 1) * MID], start=True, stop=True)
                                continue
                            m = LEVELS[n]
                            if n < WHOLE:
                                for s, o in run_pairs(m):
                                    ins = mm(lv[s:s + m, o:o + m], lev[n][:, v][:, s:s + m],
                                             lev[n][:, v][:, s + m:s + 2 * m], start=True, stop=True)
                                continue
                            ins = mm(lv.rearrange("p (g m) -> p g m", m=m), lev[n][:, v],
                                     cut(lev[n][:, v], m, 1), start=True, stop=True)
                    ins.then_inc(lev_done, 1)
                if u == 1:
                    if not first:
                        pe.wait_ge(rs_s, 2 * g)
                    pe.wait_ge(kdec_ready, g + 1)
                    for c in range(TT - 1):
                        ins = nc.tensor.transpose(XB[:, c * P:(c + 1) * P], kdec[:, c * P:(c + 1) * P], ident[:, :])
                    ins.then_inc(kt_done, 1)
                if u == 3:
                    pe.wait_ge(kt_taken, g + 1)
                    pe.wait_ge(vals_ready, g + 1)
                    for c in range(TT - 1):
                        v = slice(c * P, (c + 1) * P)
                        ins = mm(XB[:, v], kdec[:, v], vals[:, v], start=True, stop=True)
                    ins.then_inc(st_done, 1)
                if u == 5:
                    pe.wait_ge(probs_done, COPIES * (g + 1))
                    pe.wait_ge(st_v, (TT - 1) * (g + 1))
                    pe.wait_ge(qdec_ready, g + 1)
                    if not first:
                        pe.wait_ge(head_done, g)
                    for c in range(TT):
                        v = slice(c * P, (c + 1) * P)
                        ins = mm(OB[:, v], vals[:, v], probs[:, v], start=True, stop=c == 0)
                        if c:
                            ins = mm(OB[:, v], state[:, (c - 1) * P:c * P], qdec[:, v], start=False, stop=True)
                    ins.then_inc(o_done, 1)
                if u == SQ_U:
                    if last:
                        pe.wait_ge(osq_done, 2 * g + 1)
                        mm(XB, ones[:, :], t4, start=True, stop=True).then_inc(norm_done, 1)
                        return
                    pe.wait_ge(osq_done, 2 * (g + 1))
                    mm(XB, ones_r[:, :], sq_hi, start=True, stop=False)
                    mm(XB, ones_r[:, :], sq_lo, start=False, stop=True).then_inc(norm_done, 1)

            def head(h, first, second):
                for u in range(HEAD_U):
                    if u == 0:
                        pe.wait_ge(ug_taken, J) if first else pe.wait_ge(gb_taken, h)
                    if u == 2:
                        pe.wait_ge(u_taken, J) if first else pe.wait_ge(gate_taken, h)
                    if u == 4:
                        pe.wait_ge(f_v, 8 * h + 2)
                    if u == 6:
                        pe.wait_ge(q_taken, h + 1)
                    project(N_HEAD + HEAD_U * h + u, u % RING, u % 2, (u // 2) % 2)
                    if not first:
                        slot(h - 1, u, second)
                    if first and u == 4:
                        pe.wait_ge(ysum_done, J)
                        mm(bank(2), ones[:, :], lnr, start=True, stop=True).then_inc(mean_done, 1)
                    if first and u == HEAD_U - 1:
                        pe.wait_ge(vacc_done, J)
                        mm(bank(3), ones[:, :], t3, start=True, stop=True).then_inc(var_done, 1)

            head(0, True, False)
            head(1, False, True)
            with pe.Fori(2, H) as h:
                head(h, False, False)

            def out_products(c, s, tt):
                for k in range(2):
                    a = slice((2 * s + k) * T + tt * P, (2 * s + k) * T + (tt + 1) * P)
                    w = slice((s % RING) * UW + k * 512, (s % RING) * UW + (k + 1) * 512)
                    o = bank(4 * (c % 2) + tt)
                    mm(o, h_hi[:, a], w_hi[:, w], start=s == 0 and k == 0, stop=False)
                    mm(o, h_hi[:, a], w_lo[:, w], start=False, stop=False)
                    ins = mm(o, h_lo[:, a], w_hi[:, w], start=False, stop=s == OUT_U - 1 and k == 1)
                return ins

            for c in range(CHUNKS):
                for s in range(OUT_U):
                    n = N_OUT + OUT_U * c + s
                    if N_END - n <= RING:
                        break
                    if c == 0:
                        slot(H - 1, s, False, last=True)
                    if c == 0 and s == 0:
                        pe.wait_ge(gb_taken, H)
                    if s == 0 and c >= 2:
                        pe.wait_ge(y_sq, TT * (c - 1))
                    pe.wait_ge(lo_done, n + 1)
                    if c == 0:
                        pe.wait_ge(mlo_done, 2 * s + 2)
                    for tt in range(TT):
                        if (c, s, tt) == (0, 0, 1):
                            pe.wait_ge(gate_taken, H)
                        ins = out_products(c, s, tt)
                        if s == OUT_U - 1 and tt < TT - 1:
                            ins.then_inc(y_mm, 1)
                    ins.then_inc(unit_done, 1)
            for tt in range(TT):
                for s in range(OUT_U - RING, OUT_U):
                    pe.wait_ge(lo_done, N_END - OUT_U + s + 1)
                    ins = out_products(CHUNKS - 1, s, tt)
                ins.then_inc(y_mm, 1)


_INS = ["x", "pre_norm_g", "post_norm_g", "w_in", "lb_logits", "hg_norm_g", "dw_kernel", "dw_bias",
        "conv_ln_g", "conv_ln_b", "w_out"]


def kernel(**inputs):
    import numpy as np
    import concourse.bacc as bacc
    from concourse.bass_utils import run_bass_kernel_spmd

    nc = bacc.Bacc("TRN2", target_bir_lowering=False, num_devices=1)
    arrays, args = {}, []
    for name in _INS:
        a = np.ascontiguousarray(inputs[name])
        arrays[f"in_{name}"] = a
        args.append(nc.dram_tensor(f"in_{name}", a.shape, mybir.dt.from_np(a.dtype), kind="ExternalInput").ap())
    shape = inputs["x"].shape
    args.append(nc.dram_tensor("out_y", shape, mybir.dt.float32, kind="ExternalOutput").ap())
    build_layer(nc, *args)
    r = run_bass_kernel_spmd(nc, [arrays], core_ids=[0])
    return r.results[0]["out_y"]
```
